# Optimizing a Trainium2 kernel written in Bass

```python
import math
import jax, jax.numpy as jnp
from jax import lax
import numpy as np

D_MODEL = 1024
BATCH = 1
SEQ = 512
DEPTH = 2

GRID_W = 64
CTX_LEN = 256
N_MIXERS = 4
Q_BLOCK = 128
ROPE_BASE = 10000.0
EPS = 1e-6
F32 = jnp.float32

MLA_HEADS = 16
MLA_Q_RANK = 384
MLA_KV_RANK = 256
MLA_NOPE = 64
MLA_ROPE = 32
MLA_V = 64
MLA_WIDTH = MLA_HEADS * MLA_V

GLA_HEADS = 4
GLA_DK = D_MODEL // 2
GLA_DV = D_MODEL
GLA_GATE_RANK = 16
GLA_GATE_NORM = 16.0
GLA_CHUNK = 64

GQA_HEADS = 16
GQA_KV_HEADS = 4
GQA_HEAD_DIM = 64
GQA_WIDTH = GQA_HEADS * GQA_HEAD_DIM

SSD_INNER = 2 * D_MODEL
SSD_HEAD_DIM = 64
SSD_HEADS = SSD_INNER // SSD_HEAD_DIM
SSD_GROUPS = 4
SSD_STATE = 128
SSD_CONV = 5
SSD_CHUNK = 64
SSD_XBC = SSD_INNER + 2 * SSD_GROUPS * SSD_STATE


def _n_layers_of(kind):
    return len(range(kind, DEPTH, N_MIXERS))

def split_last(t, sizes):
    idx = [int(v) for v in np.cumsum(sizes)[:-1]]
    return jnp.split(t, idx, axis=-1)

def rms_norm(x, g, eps=EPS):
    xf = x.astype(F32)
    y = xf * lax.rsqrt(jnp.mean(xf * xf, axis=-1, keepdims=True) + eps)
    return (y * g.astype(F32)).astype(x.dtype)

def grid_positions(n):
    rows = n // GRID_W
    row = jnp.repeat(jnp.arange(rows, dtype=jnp.int32), GRID_W)
    col = jnp.tile(jnp.arange(GRID_W, dtype=jnp.int32), rows)
    return row, col

def _rope_1d(x, pos):
    half = x.shape[-1] // 2
    inv = ROPE_BASE ** (-jnp.arange(half, dtype=F32) / half)
    ang = pos.astype(F32)[:, None] * inv[None, :]
    cos = jnp.cos(ang)[:, None, :]
    sin = jnp.sin(ang)[:, None, :]
    xf = x.astype(F32)
    x1, x2 = xf[..., :half], xf[..., half:]
    return jnp.concatenate([x1 * cos - x2 * sin, x2 * cos + x1 * sin], axis=-1).astype(x.dtype)

def axial_rope(x, row, col):
    d = x.shape[-1] // 2
    return jnp.concatenate([_rope_1d(x[..., :d], row), _rope_1d(x[..., d:], col)], axis=-1)

def attention_blocks(q, k, v):
    b, lq, h, dk = q.shape
    hkv = k.shape[2]
    rep = h // hkv
    dv = v.shape[-1]
    scale = dk ** -0.5
    blk = min(Q_BLOCK, lq)
    nb = lq // blk
    qb = jnp.moveaxis(q.reshape(b, nb, blk, hkv, rep, dk), 1, 0)

    def one_block(qi):
        s = jnp.einsum('bqhrd,bkhd->bhrqk', qi, k, preferred_element_type=F32) * scale
        p = jax.nn.softmax(s, axis=-1).astype(v.dtype)
        return jnp.einsum('bhrqk,bkhe->bqhre', p, v)

    o = lax.map(one_block, qb)
    return jnp.moveaxis(o, 0, 1).reshape(b, lq, h, dv)

def modulation(cond, w, bias):
    m = jax.nn.silu(cond) @ w + bias
    return jnp.split(m, 3, axis=-1)

def mla_mixer(hc, hx, row, col, w_in, q_norm_g, w_uq, kv_norm_g, w_ukv, w_out):
    def project(h, rotate):
        b, n, _ = h.shape
        cq, ckv, kr, gate = split_last(h @ w_in, (MLA_Q_RANK, MLA_KV_RANK, MLA_ROPE, MLA_WIDTH))
        q = (rms_norm(cq, q_norm_g) @ w_uq).reshape(b, n, MLA_HEADS, MLA_NOPE + MLA_ROPE)
        kv = (rms_norm(ckv, kv_norm_g) @ w_ukv).reshape(b, n, MLA_HEADS, MLA_NOPE + MLA_V)
        q_nope, q_rope = q[..., :MLA_NOPE], q[..., MLA_NOPE:]
        k_nope, v = kv[..., :MLA_NOPE], kv[..., MLA_NOPE:]
        kr = kr[:, :, None, :]
        if rotate:
            q_rope = axial_rope(q_rope, row, col)
            kr = axial_rope(kr, row, col)
        k = jnp.concatenate([k_nope, jnp.broadcast_to(kr, (b, n, MLA_HEADS, MLA_ROPE))], axis=-1)
        q = jnp.concatenate([q_nope, q_rope], axis=-1)
        return q, k, v, gate

    qc, kc, vc, gc = project(hc, False)
    qx, kx, vx, gx = project(hx, True)
    oc = attention_blocks(qc, kc, vc)
    ox = attention_blocks(qx, jnp.concatenate([kc, kx], axis=1), jnp.concatenate([vc, vx], axis=1))

    def out(o, gate):
        b, n = gate.shape[:2]
        return (o.reshape(b, n, MLA_WIDTH) * jax.nn.silu(gate)) @ w_out

    return out(oc, gc), out(ox, gx)

def gla_chunk_scan(q, k, v, g, s0):
    b, l, h, dk = q.shape
    dv = v.shape[-1]
    c = GLA_CHUNK
    nc = l // c
    causal = jnp.tril(jnp.ones((c, c), dtype=bool))

    def to_chunks(t):
        return t.astype(F32).reshape(b, nc, c, h, t.shape[-1]).transpose(1, 0, 3, 2, 4)

    def step(s, inp):
        qc, kc, vc, gc = inp
        bc = jnp.cumsum(gc, axis=2)
        o_inter = jnp.einsum('bhcd,bhde->bhce', qc * jnp.exp(bc), s)
        diff = bc[:, :, :, None, :] - bc[:, :, None, :, :]
        decay = jnp.exp(jnp.where(causal[:, :, None], diff, -jnp.inf))
        a = jnp.einsum('bhid,bhijd->bhij', qc, kc[:, :, None, :, :] * decay)
        o = o_inter + jnp.einsum('bhij,bhje->bhie', a, vc)
        blast = bc[:, :, -1:, :]
        s_new = jnp.exp(blast[:, :, 0, :])[..., None] * s + jnp.einsum('bhcd,bhce->bhde', kc * jnp.exp(blast - bc), vc)
        return s_new, o

    s, o = lax.scan(step, s0, (to_chunks(q), to_chunks(k), to_chunks(v), to_chunks(g)))
    o = o.transpose(1, 0, 3, 2, 4).reshape(b, l, h, dv)
    return o, s

def gla_bidirectional(q, k, v, gf, gb, s0f, s0b):
    flip = lambda t: t[:, ::-1]
    of, sf = gla_chunk_scan(q, k, v, gf, s0f)
    ob, sb = gla_chunk_scan(flip(q), flip(k), flip(v), flip(gb), s0b)
    return of + flip(ob), sf, sb

def gla_mixer(hc, hx, w_in, w_gf, b_gf, w_gb, b_gb, o_norm_g, w_out):
    dk = GLA_DK // GLA_HEADS
    dv = GLA_DV // GLA_HEADS
    sizes = (GLA_DK, GLA_DK, GLA_DV, GLA_DV, GLA_GATE_RANK, GLA_GATE_RANK)

    def project(h):
        b, n, _ = h.shape
        q, k, v, gate, rf, rb = split_last(h @ w_in, sizes)
        heads = lambda t, d: t.reshape(b, n, GLA_HEADS, d)
        gf = jax.nn.log_sigmoid((rf @ w_gf + b_gf).astype(F32)) / GLA_GATE_NORM
        gb = jax.nn.log_sigmoid((rb @ w_gb + b_gb).astype(F32)) / GLA_GATE_NORM
        return heads(q, dk) * (dk ** -0.5), heads(k, dk), heads(v, dv), heads(gf, dk), heads(gb, dk), gate

    qc, kc, vc, gfc, gbc, gatec = project(hc)
    qx, kx, vx, gfx, gbx, gatex = project(hx)
    s0 = jnp.zeros((hc.shape[0], GLA_HEADS, dk, dv), F32)
    oc, sf, sb = gla_bidirectional(qc, kc, vc, gfc, gbc, s0, s0)
    ox, _, _ = gla_bidirectional(qx, kx, vx, gfx, gbx, sf, sb)

    def out(o, gate):
        b, n = gate.shape[:2]
        o = rms_norm(o.astype(gate.dtype), o_norm_g).reshape(b, n, GLA_DV)
        return (o * jax.nn.silu(gate)) @ w_out

    return out(oc, gatec), out(ox, gatex)

def gqa_mixer(hc, hx, row, col, w_in, q_norm_g, k_norm_g, w_out):
    kvw = GQA_KV_HEADS * GQA_HEAD_DIM

    def project(h, rotate):
        b, n, _ = h.shape
        q, k, v, gate = split_last(h @ w_in, (GQA_WIDTH, kvw, kvw, GQA_WIDTH))
        q = rms_norm(q.reshape(b, n, GQA_HEADS, GQA_HEAD_DIM), q_norm_g)
        k = rms_norm(k.reshape(b, n, GQA_KV_HEADS, GQA_HEAD_DIM), k_norm_g)
        v = v.reshape(b, n, GQA_KV_HEADS, GQA_HEAD_DIM)
        if rotate:
            q = axial_rope(q, row, col)
            k = axial_rope(k, row, col)
        return q, k, v, gate

    qc, kc, vc, gc = project(hc, False)
    qx, kx, vx, gx = project(hx, True)
    oc = attention_blocks(qc, kc, vc)
    ox = attention_blocks(qx, jnp.concatenate([kc, kx], axis=1), jnp.concatenate([vc, vx], axis=1))

    def out(o, gate):
        b, n = gate.shape[:2]
        return (o.reshape(b, n, GQA_WIDTH) * jax.nn.silu(gate)) @ w_out

    return out(oc, gc), out(ox, gx)

def dwconv_centred(u, w, bias):
    kw = w.shape[0]
    pad = kw // 2
    out = lax.conv_general_dilated(u, w[:, None, :], window_strides=(1,), padding=[(pad, kw - 1 - pad)],
                                   dimension_numbers=('NWC', 'WIO', 'NWC'), feature_group_count=u.shape[-1])
    return out + bias

def ssd_chunk_scan(x, dt, a, bm, cm, h0):
    b, l, h, p = x.shape
    g, n = bm.shape[2], bm.shape[3]
    rep = h // g
    c = SSD_CHUNK
    nc = l // c
    causal = jnp.tril(jnp.ones((c, c), dtype=bool))

    def to_chunks(t):
        return jnp.swapaxes(t.astype(F32).reshape(b, nc, c, *t.shape[2:]), 0, 1)

    def step(hs, inp):
        xc, dtc, bc, cc = inp
        la = jnp.cumsum(dtc * a, axis=1)
        xg = (xc * dtc[..., None]).reshape(b, c, g, rep, p)
        hg = hs.reshape(b, g, rep, p, n)
        y_inter = jnp.einsum('bcgn,bgrpn->bcgrp', cc, hg) * jnp.exp(la).reshape(b, c, g, rep)[..., None]
        diff = la[:, :, None, :] - la[:, None, :, :]
        lmat = jnp.exp(jnp.where(causal[None, :, :, None], diff, -jnp.inf)).reshape(b, c, c, g, rep)
        cb = jnp.einsum('bign,bjgn->bijg', cc, bc)
        y_intra = jnp.einsum('bijgr,bjgrp->bigrp', cb[..., None] * lmat, xg)
        dlast = jnp.exp(la[:, -1:, :] - la).reshape(b, c, g, rep)
        h_new = jnp.exp(la[:, -1, :]).reshape(b, g, rep)[..., None, None] * hg + \
            jnp.einsum('bcgrp,bcgn->bgrpn', dlast[..., None] * xg, bc)
        return h_new.reshape(b, h, p, n), (y_inter + y_intra).reshape(b, c, h, p)

    hs, y = lax.scan(step, h0, (to_chunks(x), to_chunks(dt), to_chunks(bm), to_chunks(cm)))
    return jnp.swapaxes(y, 0, 1).reshape(b, l, h, p), hs

def ssd_bidirectional(x, dtf, dtb, af, ab, bm, cm, h0f, h0b):
    flip = lambda t: t[:, ::-1]
    yf, hf = ssd_chunk_scan(x, dtf, af, bm, cm, h0f)
    yb, hb = ssd_chunk_scan(flip(x), flip(dtb), ab, flip(bm), flip(cm), h0b)
    return yf + flip(yb), hf, hb

def ssd_mixer(hc, hx, w_in, conv_w, conv_b, dt_bias_f, dt_bias_b, a_log_f, a_log_b, d_skip, gnorm_g, w_out):
    af = -jnp.exp(a_log_f.astype(F32))
    ab = -jnp.exp(a_log_b.astype(F32))
    gw = SSD_GROUPS * SSD_STATE

    def project(h):
        b, n, _ = h.shape
        z, xbc, dtf, dtb = split_last(h @ w_in, (SSD_INNER, SSD_XBC, SSD_HEADS, SSD_HEADS))
        xbc = jax.nn.silu(dwconv_centred(xbc, conv_w, conv_b))
        xs, bm, cm = split_last(xbc, (SSD_INNER, gw, gw))
        xs = xs.reshape(b, n, SSD_HEADS, SSD_HEAD_DIM)
        bm = bm.reshape(b, n, SSD_GROUPS, SSD_STATE)
        cm = cm.reshape(b, n, SSD_GROUPS, SSD_STATE)
        dtf = jax.nn.softplus(dtf.astype(F32) + dt_bias_f.astype(F32))
        dtb = jax.nn.softplus(dtb.astype(F32) + dt_bias_b.astype(F32))
        return z, xs, bm, cm, dtf, dtb

    zc, xsc, bmc, cmc, dtfc, dtbc = project(hc)
    zx, xsx, bmx, cmx, dtfx, dtbx = project(hx)
    h0 = jnp.zeros((hc.shape[0], SSD_HEADS, SSD_HEAD_DIM, SSD_STATE), F32)
    yc, hf, hb = ssd_bidirectional(xsc, dtfc, dtbc, af, ab, bmc, cmc, h0, h0)
    yx, _, _ = ssd_bidirectional(xsx, dtfx, dtbx, af, ab, bmx, cmx, hf, hb)

    def out(y, xs, z):
        b, n = z.shape[:2]
        y = y.astype(z.dtype) + xs * d_skip[:, None]
        y = y.reshape(b, n, SSD_INNER) * jax.nn.silu(z)
        y = rms_norm(y.reshape(b, n, SSD_GROUPS, SSD_INNER // SSD_GROUPS),
                     gnorm_g.reshape(SSD_GROUPS, SSD_INNER // SSD_GROUPS)).reshape(b, n, SSD_INNER)
        return y @ w_out

    return out(yc, xsc, zc), out(yx, xsx, zx)

def first_inputs(seed: int = 0) -> dict:
    key = jax.random.key(seed)
    ks = iter(jax.random.split(key, 64))
    nA, nB, nC, nD = (_n_layers_of(t) for t in range(N_MIXERS))

    def nrm(shape, fan_in, scale=1.0):
        return jax.random.normal(next(ks), shape, F32) * (scale * fan_in ** -0.5)

    def gain(shape):
        return 1.0 + 0.05 * jax.random.normal(next(ks), shape, F32)

    def small(shape, s=0.02):
        return s * jax.random.normal(next(ks), shape, F32)

    def dt_bias(shape):
        u = jax.random.uniform(next(ks), shape, F32)
        dt = jnp.exp(u * (math.log(0.1) - math.log(0.001)) + math.log(0.001))
        dt = jnp.maximum(dt, 1e-4)
        return dt + jnp.log(-jnp.expm1(-dt))

    def a_log(shape):
        return jnp.log(jax.random.uniform(next(ks), shape, F32, 1.0, 16.0))

    D = D_MODEL
    mla_in = MLA_Q_RANK + MLA_KV_RANK + MLA_ROPE + MLA_WIDTH
    gla_in = 2 * GLA_DK + 2 * GLA_DV + 2 * GLA_GATE_RANK
    gqa_in = 2 * GQA_WIDTH + 2 * GQA_KV_HEADS * GQA_HEAD_DIM
    ssd_in = SSD_INNER + SSD_XBC + 2 * SSD_HEADS
    return {
        "x": jax.random.normal(next(ks), (BATCH, SEQ, D), F32),
        "c": jax.random.normal(next(ks), (BATCH, D), F32),
        "ctx": jax.random.normal(next(ks), (BATCH, CTX_LEN, D), F32),
        "c_ctx": jax.random.normal(next(ks), (D,), F32),
        "ada_w": nrm((DEPTH, D, 3 * D), D, 0.5),
        "ada_b": small((DEPTH, 3 * D)),
        "norm_g": gain((DEPTH, D)),
        "final_g": gain((D,)),
        "mla_w_in": nrm((nA, D, mla_in), D),
        "mla_q_norm": gain((nA, MLA_Q_RANK)),
        "mla_w_uq": nrm((nA, MLA_Q_RANK, MLA_HEADS * (MLA_NOPE + MLA_ROPE)), MLA_Q_RANK),
        "mla_kv_norm": gain((nA, MLA_KV_RANK)),
        "mla_w_ukv": nrm((nA, MLA_KV_RANK, MLA_HEADS * (MLA_NOPE + MLA_V)), MLA_KV_RANK),
        "mla_w_out": nrm((nA, MLA_WIDTH, D), MLA_WIDTH),
        "gla_w_in": nrm((nB, D, gla_in), D),
        "gla_w_gf": nrm((nB, GLA_GATE_RANK, GLA_DK), GLA_GATE_RANK),
        "gla_b_gf": small((nB, GLA_DK), 0.1),
        "gla_w_gb": nrm((nB, GLA_GATE_RANK, GLA_DK), GLA_GATE_RANK),
        "gla_b_gb": small((nB, GLA_DK), 0.1),
        "gla_o_norm": gain((nB, GLA_DV // GLA_HEADS)),
        "gla_w_out": nrm((nB, GLA_DV, D), GLA_DV),
        "gqa_w_in": nrm((nC, D, gqa_in), D),
        "gqa_q_norm": gain((nC, GQA_HEAD_DIM)),
        "gqa_k_norm": gain((nC, GQA_HEAD_DIM)),
        "gqa_w_out": nrm((nC, GQA_WIDTH, D), GQA_WIDTH),
        "ssd_w_in": nrm((nD, D, ssd_in), D),
        "ssd_conv_w": nrm((nD, SSD_CONV, SSD_XBC), SSD_CONV),
        "ssd_conv_b": small((nD, SSD_XBC)),
        "ssd_dt_bias_f": dt_bias((nD, SSD_HEADS)),
        "ssd_dt_bias_b": dt_bias((nD, SSD_HEADS)),
        "ssd_a_log_f": a_log((nD, SSD_HEADS)),
        "ssd_a_log_b": a_log((nD, SSD_HEADS)),
        "ssd_d": gain((nD, SSD_HEADS)),
        "ssd_norm": gain((nD, SSD_INNER)),
        "ssd_w_out": nrm((nD, SSD_INNER, D), SSD_INNER),
    }

def first_block(x, c, ctx, c_ctx, ada_w, ada_b, norm_g, final_g,
              mla_w_in, mla_q_norm, mla_w_uq, mla_kv_norm, mla_w_ukv, mla_w_out,
              gla_w_in, gla_w_gf, gla_b_gf, gla_w_gb, gla_b_gb, gla_o_norm, gla_w_out,
              gqa_w_in, gqa_q_norm, gqa_k_norm, gqa_w_out,
              ssd_w_in, ssd_conv_w, ssd_conv_b, ssd_dt_bias_f, ssd_dt_bias_b,
              ssd_a_log_f, ssd_a_log_b, ssd_d, ssd_norm, ssd_w_out):
    row, col = grid_positions(x.shape[1])
    for i in range(DEPTH):
        kind, j = i % N_MIXERS, i // N_MIXERS
        sx, scx, gx = (m[:, None, :] for m in modulation(c, ada_w[i], ada_b[i]))
        sc, scc, gc = modulation(c_ctx, ada_w[i], ada_b[i])
        hx = rms_norm(x, norm_g[i]) * (1 + scx) + sx
        hc = rms_norm(ctx, norm_g[i]) * (1 + scc) + sc
        if kind == 0:
            yc, yx = mla_mixer(hc, hx, row, col, mla_w_in[j], mla_q_norm[j], mla_w_uq[j],
                               mla_kv_norm[j], mla_w_ukv[j], mla_w_out[j])
        elif kind == 1:
            yc, yx = gla_mixer(hc, hx, gla_w_in[j], gla_w_gf[j], gla_b_gf[j], gla_w_gb[j], gla_b_gb[j],
                               gla_o_norm[j], gla_w_out[j])
        elif kind == 2:
            yc, yx = gqa_mixer(hc, hx, row, col, gqa_w_in[j], gqa_q_norm[j], gqa_k_norm[j], gqa_w_out[j])
        else:
            yc, yx = ssd_mixer(hc, hx, ssd_w_in[j], ssd_conv_w[j], ssd_conv_b[j], ssd_dt_bias_f[j],
                               ssd_dt_bias_b[j], ssd_a_log_f[j], ssd_a_log_b[j], ssd_d[j], ssd_norm[j],
                               ssd_w_out[j])
        x = x + gx * yx
        if i < DEPTH - 1:
            ctx = ctx + gc * yc
    return rms_norm(x, final_g)


N_EVEN = (DEPTH + 1) // 2
N_ODD = DEPTH // 2

SSM_WIDTH = D_MODEL // 4
SSM_GROUP = 16
SSM_GROUPS = SSM_WIDTH // SSM_GROUP
SSM_STATE = 64
GMLP_WIDTH = D_MODEL - SSM_WIDTH
GMLP_HEAD = 128
GMLP_HEADS = GMLP_WIDTH // GMLP_HEAD
CHUNK = 128
EVEN_IN = SSM_WIDTH + 2 * GMLP_WIDTH

CONV_WIDTH = 3
D_FF = 2816
DT_MIN = 1e-3
DT_MAX = 1e-1
LAMBDA_RE_MAX = -1e-4
RESID_SCALE = (2 * DEPTH) ** -0.5


def rmsnorm(x, g):
    xf = x.astype(jnp.float32)
    y = xf * lax.rsqrt(jnp.mean(xf * xf, axis=-1, keepdims=True) + EPS)
    return (y * g.astype(jnp.float32)).astype(x.dtype)

def causal_dwconv(x, w, b):
    k_w = w.shape[0]
    s = x.shape[1]
    xp = jnp.pad(x, ((0, 0), (k_w - 1, 0), (0, 0)))
    return b + sum(w[k] * xp[:, k:k + s] for k in range(k_w))

def s5_mixer(u, lam_re, lam_im, log_dt, b_re, b_im, c_re, c_im, d_skip, w_glu, b_glu):
    bsz, s, _ = u.shape
    uf = u.astype(jnp.float32).reshape(bsz, s, SSM_GROUPS, SSM_GROUP)
    lr = jnp.minimum(lam_re.astype(jnp.float32), LAMBDA_RE_MAX)
    li = lam_im.astype(jnp.float32)
    dt = jnp.exp(log_dt.astype(jnp.float32))[:, None]
    mag = jnp.exp(lr * dt)
    ab_re = mag * jnp.cos(li * dt)
    ab_im = mag * jnp.sin(li * dt)
    den = lr * lr + li * li
    nr = ab_re - 1.0
    ni = ab_im
    z_re = ((nr * lr + ni * li) / den)[..., None]
    z_im = ((ni * lr - nr * li) / den)[..., None]
    br = b_re.astype(jnp.float32)
    bi = b_im.astype(jnp.float32)
    bb_re = z_re * br - z_im * bi
    bb_im = z_re * bi + z_im * br
    x_re = jnp.einsum('bsgh,gph->bsgp', uf, bb_re)
    x_im = jnp.einsum('bsgh,gph->bsgp', uf, bb_im)
    a_re = jnp.broadcast_to(ab_re, (1, s) + ab_re.shape)
    a_im = jnp.broadcast_to(ab_im, (1, s) + ab_im.shape)

    def combine(left, right):
        a1r, a1i, b1r, b1i = left
        a2r, a2i, b2r, b2i = right
        return (a2r * a1r - a2i * a1i,
                a2r * a1i + a2i * a1r,
                a2r * b1r - a2i * b1i + b2r,
                a2r * b1i + a2i * b1r + b2i)

    _, _, h_re, h_im = lax.associative_scan(combine, (a_re, a_im, x_re, x_im), axis=1)
    y = (jnp.einsum('bsgp,ghp->bsgh', h_re, c_re.astype(jnp.float32))
         - jnp.einsum('bsgp,ghp->bsgh', h_im, c_im.astype(jnp.float32)))
    y = (y + d_skip.astype(jnp.float32).reshape(SSM_GROUPS, SSM_GROUP) * uf).reshape(bsz, s, SSM_WIDTH)
    y = jax.nn.gelu(y)
    y = y * jax.nn.sigmoid(y @ w_glu.astype(jnp.float32) + b_glu.astype(jnp.float32))
    return y.astype(u.dtype)

def gmlp_mixer(uv, w_s, b_s, g_v):
    bsz, s, _ = uv.shape
    u, v = jnp.split(jax.nn.gelu(uv), 2, axis=-1)
    v = rmsnorm(v, g_v).reshape(bsz, s // CHUNK, CHUNK, GMLP_HEADS, GMLP_HEAD)
    mask = jnp.tril(jnp.ones((CHUNK, CHUNK), dtype=bool))
    w = jnp.where(mask, w_s, 0)
    gate = jnp.einsum('hts,bnshc->bnthc', w, v) + b_s.T[None, None, :, :, None]
    return u * gate.reshape(bsz, s, GMLP_WIDTH)

def shortconv_mixer(p, w_conv, b_conv):
    bg, cg, hx = jnp.split(p, 3, axis=-1)
    return bg * causal_dwconv(cg * hx, w_conv, b_conv)

def conv_ffn(x, w_up, w_conv, b_conv, w_down):
    h = causal_dwconv(x @ w_up, w_conv, b_conv)
    gate, val = jnp.split(h, 2, axis=-1)
    return (jax.nn.silu(gate) * val) @ w_down

def second_inputs(seed: int = 0) -> dict:
    key = jax.random.key(seed)
    ks = iter(jax.random.split(key, 32))
    f32 = jnp.float32
    nrm = lambda shape, std: std * jax.random.normal(next(ks), shape, f32)
    d = D_MODEL
    inp = {}
    inp["x"] = nrm((BATCH, SEQ, d), 1.0)
    inp["mix_norm_g"] = 1.0 + nrm((DEPTH, d), 0.02)
    inp["ffn_norm_g"] = 1.0 + nrm((DEPTH, d), 0.02)
    inp["final_norm_g"] = 1.0 + nrm((d,), 0.02)
    inp["ev_w_in"] = nrm((N_EVEN, d, EVEN_IN), d ** -0.5)
    inp["ev_w_out"] = nrm((N_EVEN, d, d), d ** -0.5 * RESID_SCALE)
    inp["s5_lam_re"] = -0.5 + nrm((N_EVEN, SSM_GROUPS, SSM_STATE), 0.01)
    n_idx = jnp.arange(SSM_STATE, dtype=f32)
    inp["s5_lam_im"] = math.pi * n_idx + nrm((N_EVEN, SSM_GROUPS, SSM_STATE), 0.01)
    inp["s5_log_dt"] = jax.random.uniform(next(ks), (N_EVEN, SSM_GROUPS), f32,
                                          math.log(DT_MIN), math.log(DT_MAX))
    inp["s5_b_re"] = nrm((N_EVEN, SSM_GROUPS, SSM_STATE, SSM_GROUP), (2 * SSM_GROUP) ** -0.5)
    inp["s5_b_im"] = nrm((N_EVEN, SSM_GROUPS, SSM_STATE, SSM_GROUP), (2 * SSM_GROUP) ** -0.5)
    inp["s5_c_re"] = nrm((N_EVEN, SSM_GROUPS, SSM_GROUP, SSM_STATE), SSM_STATE ** -0.5)
    inp["s5_c_im"] = nrm((N_EVEN, SSM_GROUPS, SSM_GROUP, SSM_STATE), SSM_STATE ** -0.5)
    inp["s5_d"] = nrm((N_EVEN, SSM_WIDTH), 1.0)
    inp["s5_w_glu"] = nrm((N_EVEN, SSM_WIDTH, SSM_WIDTH), SSM_WIDTH ** -0.5)
    inp["s5_b_glu"] = nrm((N_EVEN, SSM_WIDTH), 0.01)
    inp["gm_w_s"] = nrm((N_EVEN, GMLP_HEADS, CHUNK, CHUNK), CHUNK ** -0.5)
    inp["gm_b_s"] = 1.0 + nrm((N_EVEN, GMLP_HEADS, CHUNK), 0.01)
    inp["gm_v_g"] = 1.0 + nrm((N_EVEN, GMLP_WIDTH), 0.02)
    inp["od_w_in"] = nrm((N_ODD, d, 3 * d), d ** -0.5)
    inp["od_conv_w"] = nrm((N_ODD, CONV_WIDTH, d), CONV_WIDTH ** -0.5)
    inp["od_conv_b"] = nrm((N_ODD, d), 0.01)
    inp["od_w_out"] = nrm((N_ODD, d, d), d ** -0.5 * RESID_SCALE)
    inp["ffn_w_up"] = nrm((DEPTH, d, 2 * D_FF), d ** -0.5)
    inp["ffn_conv_w"] = nrm((DEPTH, CONV_WIDTH, 2 * D_FF), CONV_WIDTH ** -0.5)
    inp["ffn_conv_b"] = nrm((DEPTH, 2 * D_FF), 0.01)
    inp["ffn_w_down"] = nrm((DEPTH, D_FF, d), D_FF ** -0.5 * RESID_SCALE)
    return inp

def second_block(x, mix_norm_g, ffn_norm_g, final_norm_g,
              ev_w_in, ev_w_out, s5_lam_re, s5_lam_im, s5_log_dt,
              s5_b_re, s5_b_im, s5_c_re, s5_c_im, s5_d, s5_w_glu, s5_b_glu,
              gm_w_s, gm_b_s, gm_v_g,
              od_w_in, od_conv_w, od_conv_b, od_w_out,
              ffn_w_up, ffn_conv_w, ffn_conv_b, ffn_w_down):
    h = x
    for layer in range(DEPTH):
        y = rmsnorm(h, mix_norm_g[layer])
        if layer % 2 == 0:
            e = layer // 2
            p = y @ ev_w_in[e]
            a_out = s5_mixer(p[..., :SSM_WIDTH], s5_lam_re[e], s5_lam_im[e], s5_log_dt[e],
                             s5_b_re[e], s5_b_im[e], s5_c_re[e], s5_c_im[e],
                             s5_d[e], s5_w_glu[e], s5_b_glu[e])
            b_out = gmlp_mixer(p[..., SSM_WIDTH:], gm_w_s[e], gm_b_s[e], gm_v_g[e])
            mix = jnp.concatenate([a_out, b_out], axis=-1) @ ev_w_out[e]
        else:
            o = layer // 2
            mix = shortconv_mixer(y @ od_w_in[o], od_conv_w[o], od_conv_b[o]) @ od_w_out[o]
        h = h + mix
        h = h + conv_ffn(rmsnorm(h, ffn_norm_g[layer]), ffn_w_up[layer], ffn_conv_w[layer],
                         ffn_conv_b[layer], ffn_w_down[layer])
    return rmsnorm(h, final_norm_g)


_first_inputs = second_inputs


def second_inputs(seed=0):
    import zlib

    import numpy as np

    out = dict(_first_inputs(seed))
    spreads = {}
    factors = {'mix_norm_g': 3.036,
     'ffn_norm_g': 26.233,
     'final_norm_g': 26.915,
     's5_lam_re': 64.0,
     's5_lam_im': 60.64,
     's5_log_dt': 61.936,
     's5_b_re': 64.0,
     's5_b_im': 64.0,
     's5_c_re': 64.0,
     's5_c_im': 64.0,
     's5_b_glu': 200.0,
     'gm_b_s': 173.73,
     'gm_v_g': 121.287,
     'od_conv_b': 61.643,
     'ffn_conv_b': 53.176,
     's5_d': 4.977,
     's5_w_glu': 8.0}
    for name, (base, spread) in spreads.items():
        noise = np.random.default_rng([zlib.crc32(name.encode()), seed]).standard_normal(out[name].shape)
        drawn = base * np.exp(spread * noise) if base else spread * noise
        out[name] = __import__('jax').numpy.asarray(drawn.astype(out[name].dtype))
    for name, factor in factors.items():
        out[name] = (out[name] * factor).astype(out[name].dtype)
    return out


_narrow_inputs = second_inputs


def second_inputs(seed=0):
    out = dict(_narrow_inputs(seed))
    wider = {'final_norm_g': 3.38,
     's5_d': 4.14,
     's5_w_glu': 5.53,
     's5_b_glu': 12.0,
     'gm_b_s': 5.03,
     'gm_v_g': 4.97,
     'od_conv_b': 12.0}
    for name, times in wider.items():
        mean = out[name].mean()
        out[name] = (mean + times * (out[name] - mean)).astype(out[name].dtype)
    return out


def setup_inputs(seed=0):
    out = dict(first_inputs(seed))
    for name, value in second_inputs(seed + 1).items():
        if name != "x":
            out[name + "_2"] = value
    return out


def reference(
    x, c, ctx, c_ctx, ada_w, ada_b, norm_g, final_g, mla_w_in, mla_q_norm, mla_w_uq,
    mla_kv_norm, mla_w_ukv, mla_w_out, gla_w_in, gla_w_gf, gla_b_gf, gla_w_gb, gla_b_gb,
    gla_o_norm, gla_w_out, gqa_w_in, gqa_q_norm, gqa_k_norm, gqa_w_out, ssd_w_in, ssd_conv_w,
    ssd_conv_b, ssd_dt_bias_f, ssd_dt_bias_b, ssd_a_log_f, ssd_a_log_b, ssd_d, ssd_norm,
    ssd_w_out, mix_norm_g_2, ffn_norm_g_2, final_norm_g_2, ev_w_in_2, ev_w_out_2, s5_lam_re_2,
    s5_lam_im_2, s5_log_dt_2, s5_b_re_2, s5_b_im_2, s5_c_re_2, s5_c_im_2, s5_d_2, s5_w_glu_2,
    s5_b_glu_2, gm_w_s_2, gm_b_s_2, gm_v_g_2, od_w_in_2, od_conv_w_2, od_conv_b_2, od_w_out_2,
    ffn_w_up_2, ffn_conv_w_2, ffn_conv_b_2, ffn_w_down_2,
):
    x = first_block(
        x, c, ctx, c_ctx, ada_w, ada_b, norm_g, final_g, mla_w_in, mla_q_norm, mla_w_uq,
        mla_kv_norm, mla_w_ukv, mla_w_out, gla_w_in, gla_w_gf, gla_b_gf, gla_w_gb, gla_b_gb,
        gla_o_norm, gla_w_out, gqa_w_in, gqa_q_norm, gqa_k_norm, gqa_w_out, ssd_w_in,
        ssd_conv_w, ssd_conv_b, ssd_dt_bias_f, ssd_dt_bias_b, ssd_a_log_f, ssd_a_log_b, ssd_d,
        ssd_norm, ssd_w_out,
    )
    return second_block(
        x, mix_norm_g_2, ffn_norm_g_2, final_norm_g_2, ev_w_in_2, ev_w_out_2, s5_lam_re_2,
        s5_lam_im_2, s5_log_dt_2, s5_b_re_2, s5_b_im_2, s5_c_re_2, s5_c_im_2, s5_d_2,
        s5_w_glu_2, s5_b_glu_2, gm_w_s_2, gm_b_s_2, gm_v_g_2, od_w_in_2, od_conv_w_2,
        od_conv_b_2, od_w_out_2, ffn_w_up_2, ffn_conv_w_2, ffn_conv_b_2, ffn_w_down_2,
    )


_drawn_inputs = setup_inputs


def setup_inputs(seed=0):
    import zlib

    import numpy as np

    out = dict(_drawn_inputs(seed))
    spreads = {}
    factors = {'mla_q_norm': 8.0,
     'mla_kv_norm': 8.0,
     'gla_b_gf': 4.978,
     'gla_b_gb': 5.019,
     'gla_o_norm': 3.257,
     's5_b_glu_2': 31.568}
    for name, (base, spread) in spreads.items():
        noise = np.random.default_rng([zlib.crc32(name.encode()), seed]).standard_normal(out[name].shape)
        drawn = base * np.exp(spread * noise) if base else spread * noise
        out[name] = __import__('jax').numpy.asarray(drawn.astype(out[name].dtype))
    for name, factor in factors.items():
        out[name] = (out[name] * factor).astype(out[name].dtype)
    return out
```

```python
from contextlib import ExitStack

import numpy as np

import concourse.bass as bass
from concourse import mybir

D, T, TC = 1024, 512, 256
N = T + TC
P = 128
KD = D // P
TX, TCX, TN = T // P, TC // P, N // P
H, NOPE, ROPE, HV = 16, 64, 32, 64
QR, KVR = 384, 256
GH, GK, GV = 4, 128, 256
GATE_NORM = 16.0
LEVELS = [1, 2, 4, 8, 16, 32, 64]
SG = 8
SW = D // 4
GM = 6
DFF = 2816
FH = DFF // P // 2
EPS = 1e-6
UT = 8
RAW, CONV = 5, 3
BANKS2 = 4

VECS = [("cond", 16), ("ada_b0", 48), ("ada_b1", 48), ("norm_g0", 16), ("norm_g1", 16),
        ("final_g", 8), ("q_g", 3), ("kv_g", 2), ("b_gf", 4), ("b_gb", 4), ("o_g", 2),
        ("mix_g0", 8), ("mix_g1", 8), ("ffn_g0", 8), ("ffn_g1", 8), ("final_g2", 8),
        ("lam_re", 8), ("lam_im", 8), ("log_dt", 8), ("s5_d", 2), ("b_glu", 2), ("v_g", 6),
        ("od_w", 24), ("od_b", 8), ("ffn_w0", 132), ("ffn_w1", 132), ("ffn_b0", 44), ("ffn_b1", 44)]
VAT, _at = {}, 0
for _n, _w in VECS:
    VAT[_n] = (_at, _w)
    _at += _w
NV = _at

NORMS = [("n0", 8, D, N), ("cq", 3, QR, N), ("ckv", 2, KVR, N), ("n1", 8, D, N)]
NORMS += [(f"o{h}", 2, GV, T) for h in range(GH)]
NORMS += [(n, 8, D, T) for n in ("f1", "mix0", "ffn0", "mix1", "ffn1", "f2")]
NI = {n[0]: i for i, n in enumerate(NORMS)}
NK = [sum(n[1] for n in NORMS[:i]) for i in range(len(NORMS) + 1)]
NA = [sum(n[1] - 1 for n in NORMS[:i]) for i in range(len(NORMS) + 1)]

SPLITS = [("n0", 8), ("cq", 3), ("ckv", 2), ("attn", 8), ("n1", 8)]
SPLITS += [(f"o{h}", 2) for h in range(GH)]
SPLITS += [("mix0", 8), ("gm", 6), ("s5", 2)]
for _l in range(2):
    SPLITS += ([("mix1", 8), ("od", 8)] if _l else [])
    SPLITS += [(f"ffn{_l}", 8), (f"act{_l}0", FH), (f"act{_l}1", FH)]
SAT, _at = {}, 0
for _n, _w in SPLITS:
    SAT[_n] = _at
    _at += _w

RESID = ["l0", "l1", "f1", "ev", "f00", "f01", "od", "f10", "f11"]
RAT = {n: 8 * i for i, n in enumerate(RESID)}

UNITS = [(h, q) for h in range(H) for q in range(TN)]
NU = len(UNITS)


def unit_keys(q):
    return list(range(TN)) if q < TX else list(range(TX, TN))


LOG_EXP = "natural_log_exp_and_others"
EV_K = [2, 3, 4, 5, 6, 7, 0, 1]


class Plan:

    def __init__(self):
        self.index, self.free, self.first, self.count = {}, [], [], []
        self.split, self.units, self.ada = [], [], 0
        self.last = {}
        n = 0

        def tile(key, free, weights=(), again=None):
            self.index[key] = len(self.free)
            self.free.append(free)
            start = len(self.split)
            if again is not None:
                start, weights_n = self.first[self.index[again]], self.count[self.index[again]]
            else:
                weights_n = len(weights)
                for w in weights:
                    if len(self.split) % UT == 0:
                        self.units.append(("split", len(self.split) // UT))
                    self.split.append(w)
            self.first.append(start)
            self.count.append(weights_n)
            for i in range(start, start + weights_n):
                self.last[("split", i // UT)] = len(self.free) - 1

        def ada(layer, j):
            for half in range(2):
                self.units.append(("raw", self.ada))
                self.last[("raw", self.ada)] = len(self.free)
                self.ada += 1
            tile(("ada", layer, j), [("mod", 12 * layer + j + 1)])

        def ktiles(name, m, k=KD):
            return [(name, i, m) for i in range(k)]

        def norm(name):
            tile(("ss", name), [("n_rs", 2 * NI[name] + 1)])

        for j in range(8):
            ada(0, j)
        norm("n0")
        for m in range(5):
            tile(("c", m), [("craw", m + 1)], ktiles("win0", m))
        tile("kr", [("kr", 4)], ktiles("win0", 5))
        for m in range(8):
            tile(("gate0", m), [("gate0", m + 1)], ktiles("win0", 6 + m))
            if m == 1:
                norm("cq")
            if m == 3:
                norm("ckv")
        vt = [("uv", k, m) for k in range(2) for m in range(8)]
        for t in range(TN):
            tile(("v", t), [("v", t + 1)], vt, None if t == 0 else ("v", 0))

        def qk(h):
            tile(("Q", h), [("q_nope", h + 1), ("q_rope", 4 * h + 4)], [("uq", k, h) for k in range(3)])
            tile(("K", h), [("k_nope", h + 1)], [("uk", k, h) for k in range(2)])

        def score(u):
            tile(("S", u), [("p", u + 1)])

        more = [(0, j) for j in range(8, 12)] + [(1, j) for j in range(12)]
        qk(0)
        score(0)
        score(1)
        for u in range(NU):
            if u % TN == 1 and u // TN + 1 < H:
                qk(u // TN + 1)
            if u % TN == 3:
                ada(*more.pop(0))
            if u + 2 < NU:
                score(u + 2)
            tile(("PT", u), [("pt", u + 1)])
            if u:
                tile(("O", u - 1), [("o", u)])
        tile(("O", NU - 1), [("o", NU)])
        for m in range(8):
            tile(("OT", m), [("hf", SAT["attn"] + m + 1)])
        for m in range(8):
            tile(("l0", m), [("residc", m + 1)], ktiles("wout0", m))
        norm("n1")
        tile("r", [("gr", 1)], ktiles("gr", 0))
        for h in range(GH):
            tile(("gq", h), [("gq", h + 1)], ktiles("gin", h))
            tile(("gk", h), [("gk", h + 1)], ktiles("gin", 4 + h))
            tile(("gf", h), [("g_min", 2 * h + 1), ("g_log", 6 * h + 1)])
            tile(("gb", h), [("g_min", 2 * h + 2), ("g_log", 6 * h + 4)])
            w = [("gin", k, 8 + 2 * h + m) for k in range(KD) for m in range(2)]
            for t in range(2):
                tile(("gv", h, t), [("gv", 2 * h + t + 1)], w, None if t == 0 else ("gv", h, 0))
            for m in range(2):
                tile(("gg", h, m), [("gg", 2 * h + m + 1)], ktiles("gin", 16 + 2 * h + m))
            for l in range(8):
                tile(("lev", h, l), [("lev", 15 * h + max(1, 2 * l))])
            for d in range(2):
                tile(("kT", h, d), [("kT", 2 * h + d + 1)])
                tile(("st", h, d), [("st", 8 * h + 4 * d + 4)])
            for m in range(2):
                tile(("go", h, m), [("go", 2 * h + m + 1)])
            norm(f"o{h}")
        for m in range(8):
            tile(("l1", m), [("resid", RAT["l1"] + m + 1)], ktiles("wout1", m))
        norm("f1")
        norm("mix0")
        for m in range(2):
            tile(("su", m), [("su", m + 1)], ktiles("ein", m))
        for w in range(3):
            wt = [("ein", k, 8 + 2 * w + m) for k in range(KD) for m in range(2)]
            tile(("mv", w), [("mv", w + 1)], wt)
            for j in range(2 * w, 2 * w + 2):
                tile(("sx", j), [("sx", j + 1)])
        for m in range(GM):
            tile(("mu", m), [("mu", m + 1)], ktiles("ein", 2 + m))
            if m < 2:
                tile(("sx", 6 + m), [("sx", 7 + m)])
        for m in range(GM):
            tile(("mg", m), [("mg", m + 1)])
        for c in range(2):
            tile(("sy", c), [("sy", c + 1)])
        for c in range(2):
            tile(("glu", c), [("glu", c + 1)])
        for m in range(8):
            tile(("ev", m), [("resid", RAT["ev"] + m + 1)],
                 [("eout", k, m) for k in EV_K])

        def ffn(l):
            norm(f"ffn{l}")
            for f in range(2):
                for j in range(FH):
                    tile(("up", l, f, j), [("conv", 4 * ((2 * l + f) * FH + j + 1))],
                         ktiles(f"up{l}", f * FH + j) + ktiles(f"up{l}", 2 * FH + f * FH + j))
                for m in range(8):
                    tile(("dn", l, f, m), [("resid", RAT[f"f{l}{f}"] + m + 1)],
                         [(f"dn{l}", f * FH + k, m) for k in range(FH)])

        ffn(0)
        norm("mix1")
        for m in range(8):
            tile(("ch", m), [("ch", m + 1)], ktiles("oin", 8 + m) + ktiles("oin", 16 + m))
            tile(("bg", m), [("hf", SAT["od"] + m + 1)], ktiles("oin", m))
        for m in range(8):
            tile(("od", m), [("resid", RAT["od"] + m + 1)], ktiles("oout", m))
        ffn(1)
        norm("f2")
        self.nsplit = -(-len(self.split) // UT)
        self.unit_at = {u: i for i, u in enumerate(self.units)}
        self.load_after, most = [], -1
        for c in range(len(self.units)):
            if c >= RAW and self.units[c - RAW][0] == "raw":
                most = max(most, self.last[self.units[c - RAW]])
            self.load_after.append(most)
        self.first_use = {}
        for n, (s, c) in enumerate(zip(self.first, self.count, strict=True)):
            for i in range(s, s + c):
                self.first_use.setdefault(i // UT, n)


PLAN = Plan()



class Serial:

    def __init__(self, engine, sem, own):
        self.engine, self.sem, self.own, self.counts = engine, sem, own, {}

    def __call__(self, instruction, name=None):
        name = name or self.own
        self.counts[name] = self.counts.get(name, 0) + 1
        instruction.then_inc(self.sem(name), 1)
        self.engine.wait_ge(self.sem(name), self.counts[name])


def hf_of(j):
    return SAT[f"act{j // (2 * FH)}{j // FH % 2}"] + j % FH + 1


def build(nc, a):
    fp32, fp22 = mybir.dt.float32, mybir.dt.float32r
    ALU, ACT, AX = mybir.AluOpType, mybir.ActivationFunctionType, mybir.AxisListType
    plan = PLAN
    ctx = ExitStack()
    sems = {}

    def sem(name):
        if name not in sems:
            sems[name] = ctx.enter_context(nc.semaphore("s_" + name))
        return sems[name]

    def sb(name, shape, dt=fp32):
        return ctx.enter_context(nc.sbuf_tensor(name, [P] + shape, dt))

    def place(at, name, shape, dt=fp32):
        scope = ExitStack()
        if at:
            scope.enter_context(nc.sbuf_tensor(f"before_{name}", [P, at], fp32))
        t = scope.enter_context(nc.sbuf_tensor(name, [P] + shape, dt))
        scope.close()
        return t

    with ctx:
        PS = [ctx.enter_context(nc.psum_tensor(f"ps{i}", [P, 1024], fp32)) for i in range(BANKS2)]
        raw = sb("raw", [RAW, UT * P])
        whi, wlo = sb("whi", [CONV, UT * P], fp22), sb("wlo", [CONV, UT * P], fp22)
        X = sb("X", [KD, T])
        vec = sb("vec", [NV])
        ident, ones = sb("ident", [P]), sb("ones", [2 * P])
        hf = sb("hf", [2, N])
        sq = sb("sq", [3, N])
        acc, rstd = sb("acc", [N]), sb("rstd", [N])
        small2 = sb("small2", [2])
        eps1 = sb("eps1", [2])
        mod = sb("mod", [2, 48])
        sc1 = sb("sc1", [2, 16])
        cnd = sb("cnd", [16])
        CX = place(0, "CX", [KD, TC])
        rope = place(2048, "rope", [T])
        gate0 = place(2560, "gate0", [KD, N])
        Hhi, Hlo = place(8704, "Hhi", [KD, N], fp22), place(14848, "Hlo", [KD, N], fp22)
        V, O = place(8704, "V", [TN, D]), place(14848, "O", [TN, D])
        Chi, Clo = place(20992, "Chi", [5, N], fp22), place(24832, "Clo", [5, N], fp22)
        craw = place(28672, "craw", [5, N])
        Q, Pr, PT, K = (place(28672 + 1536 * i, n, [2, N]) for i, n in enumerate(["Q", "Pr", "PT", "K"]))
        small = place(34816, "small", [3, 8])
        Ahi, Alo = place(20992, "Ahi", [KD, N], fp22), place(27136, "Alo", [KD, N], fp22)
        gR, masks = place(33280, "gR", [N]), place(34048, "masks", [8, P])
        ghi, glo = place(2048, "ghi", [KD, T], fp22), place(6144, "glo", [KD, T], fp22)
        wg = place(10240, "wg", [2, 512])
        gv, S = place(11264, "gv", [TN, GV]), place(12800, "S", [2, 4, GV])
        ex = place(14848, "ex", [2, 2, T])
        gk, bF, nB = (place(16896 + N * i, n, [N]) for i, n in enumerate(["gk", "bF", "nB"]))
        kT = place(19200, "kT", [N])
        gG = place(19968, "gG", [2, T])
        gq, At, Am = (place(T * i, n, [T]) for i, n in enumerate(["gq", "At", "Am"]))
        edge = place(3 * T, "edge", [20])
        Fhi, Flo = place(0, "Fhi", [FH, T], fp22), place(5632, "Flo", [FH, T], fp22)
        cv = place(11264, "cv", [3, 2, T])
        tmp = place(33280, "tmp", [2, 2 * T])
        lB, lC = place(0, "lB", [2, 2, P]), place(512, "lC", [2, SG, 32])
        glw = place(1024, "glw", [2, SW])
        gmw, bs = place(1536, "gmw", [GM, P]), place(2304, "bs", [GM, P])
        tab = place(3072, "tab", [2, SG, P])
        sp = place(5120, "sp", [32, SG])
        U = place(5376, "U", [2, T])
        mV, mU = place(6400, "mV", [TX, GM * P]), place(9472, "mU", [GM, T])
        wS = place(12544, "wS", [SG, 2, T])
        mst = place(20736, "mst", [TX])
        wtmp = sq[:, :, :].rearrange("p a t -> p (a t)")[:, 0:2 * T]

        def v_(name, i=0, n=1):
            return vec[:, VAT[name][0] + i:VAT[name][0] + i + n]

        block = ctx.enter_context(nc.Block())

        @block.sync
        def _(sy):
            ns = {}
            for c, (kind, i) in enumerate(plan.units):
                if c >= RAW:
                    was, j = plan.units[c - RAW]
                    if was == "split":
                        sy.wait_ge(sem("wlo"), j + 1)
                    else:
                        sy.wait_ge(sem("psum"), plan.last[(was, j)] + 1)
                sy.dma_start(raw[:, c % RAW, :], a["units"][c]).then_inc(sem(f"ld{c % RAW}"), 16)
            for k in range(KD):
                sy.wait_ge(sem("out"), k + 1)
                sy.dma_start(a["out"][:, k, :], X[:, k, :]).then_inc(sem("stored"), 16)
            sy.wait_ge(sem("stored"), 16 * KD)

        @block.gpsimd
        def _(po):
            masked = False
            for s in range(plan.nsplit):
                po.wait_ge(sem("whi"), s + 1)
                nc.gpsimd.tensor_tensor(wlo[:, s % CONV, :], raw[:, plan.unit_at[("split", s)] % RAW, :],
                                        whi[:, s % CONV, :].bitcast(fp32), ALU.subtract).then_inc(sem("wlo"), 1)
                if not masked and s * UT >= plan.first[plan.index[("mv", 0)]]:
                    masked = True
                    po.wait_ge(sem("evc"), 16 * 5)
                    nc.gpsimd.affine_select(out=gmw[:, :, :], in_=gmw[:, :, :], compare_op=ALU.is_ge, fill=0.0,
                                            base=0, pattern=[[0, GM], [1, P]], channel_multiplier=-1)\
                        .then_inc(sem("gmw"), 1)

        @block.tensor
        def _(pe):
            at = [0]

            def tile(key):
                n = plan.index[key]
                assert n == at[0], (key, n, at[0])
                at[0] += 1
                if n >= BANKS2:
                    for name, value in plan.free[n - BANKS2]:
                        pe.wait_ge(sem(name), value)
                return PS[n % BANKS2]

            def done(last):
                last.then_inc(sem("psum"), 1)

            seen = [-1]

            def weights(key, i, n=P):
                w = plan.first[plan.index[key]] + i
                s, j = w // UT, w % UT
                if s > seen[0]:
                    pe.wait_ge(sem("wlo"), s + 1)
                    seen[0] = s
                return (x[:, s % CONV, j * P:j * P + n] for x in (whi, wlo))

            def product(out, stat, mov, first, last):
                (sh, sl), (mh, ml) = stat, mov
                nc.tensor.matmul(out, sh, mh, start=first, stop=False)
                nc.tensor.matmul(out, sh, ml, start=False, stop=False)
                return nc.tensor.matmul(out, sl, mh, start=False, stop=last)

            def linear(key, hi, lo, k_at, ready, cols, offset=0, ks=None, col0=0):
                ps = PS[plan.index[key] % BANKS2]
                ks = ks or list(range(plan.count[plan.index[key]]))
                for i, k in enumerate(ks):
                    if ready is not None:
                        pe.wait_ge(sem("lo"), ready + i)
                    w = tuple(weights(key, offset + i))
                    for c0, c1 in cols:
                        last = product(ps[:, col0 + c0:col0 + c1], w, (hi[:, k_at + k, c0:c1], lo[:, k_at + k, c0:c1]),
                                       i == 0, i == len(ks) - 1)
                return last

            def norm(name):
                _, k, _, n = NORMS[NI[name]]
                ps = tile(("ss", name))
                pe.wait_ge(sem("n_acc"), NA[NI[name] + 1])
                for c0 in range(0, n, T):
                    last = nc.tensor.matmul(ps[:, c0:min(n, c0 + T)], ones[:, 0:P], acc[:, c0:min(n, c0 + T)],
                                            start=True, stop=True)
                done(last)

            def ada(layer, j):
                ps = tile(("ada", layer, j))
                for m in range(2):
                    n = 24 * layer + 2 * j + m
                    c = plan.unit_at[("raw", n)]
                    pe.wait_ge(sem(f"ld{c % RAW}"), 16 * (c // RAW + 1))
                    for k in range(KD):
                        last = nc.tensor.matmul(ps[:, 2 * m:2 * m + 2], raw[:, c % RAW, k * P:(k + 1) * P],
                                                cnd[:, 2 * k:2 * k + 2], start=k == 0, stop=k == KD - 1)
                done(last)

            BOTH, XO = [(0, T), (T, N)], [(0, T)]
            pe.wait_ge(sem("cnd"), 1)
            for j in range(8):
                ada(0, j)
            pe.wait_ge(sem("consts"), 16 * 4)
            pe.wait_ge(sem("ones"), 2)
            norm("n0")
            for m in range(5):
                tile(("c", m))
                done(linear(("c", m), Hhi, Hlo, 0, SAT["n0"] + 1, BOTH))
            tile("kr")
            done(linear("kr", Hhi, Hlo, 0, None, BOTH))
            for m in range(8):
                tile(("gate0", m))
                done(linear(("gate0", m), Hhi, Hlo, 0, None, BOTH))
                if m == 1:
                    norm("cq")
                if m == 3:
                    norm("ckv")
            pe.wait_ge(sem("lo"), SAT["ckv"] + 2)
            for t in range(TN):
                ps = tile(("v", t))
                for half in range(2):
                    for k in range(2):
                        w = tuple(weights(("v", t), 8 * k + 4 * half, 512))
                        tok = tuple(x[:, 3 + k, t * P:(t + 1) * P] for x in (Chi, Clo))
                        last = product(ps[:, 512 * half:512 * half + 512], tok, w, k == 0, k == 1)
                done(last)

            def qk(h):
                tile(("Q", h))
                done(linear(("Q", h), Chi, Clo, 0, None, BOTH))
                tile(("K", h))
                done(linear(("K", h), Chi, Clo, 3, None, BOTH))

            def score(u):
                h, q = UNITS[u]
                ps = tile(("S", u))
                if q == 0:
                    pe.wait_ge(sem("q_nope"), h + 1)
                    pe.wait_ge(sem("q_rope"), 4 * h + 4)
                    pe.wait_ge(sem("k_nope"), h + 1)
                    pe.wait_ge(sem("kr"), 6)
                for c0, c1 in (BOTH if q < TX else [(T, N)]):
                    o0 = c0 if q < TX else 0
                    last = nc.tensor.matmul(ps[:, o0:o0 + c1 - c0], Q[0:96, h % 2, q * P:(q + 1) * P],
                                            K[0:96, h % 2, c0:c1], start=True, stop=True)
                done(last)

            def out(u):
                h, q = UNITS[u]
                ps = tile(("O", u))
                pe.wait_ge(sem("pt"), u + 1)
                keys = unit_keys(q)
                for i, t in enumerate(keys):
                    last = nc.tensor.matmul(ps[:, 0:HV], PT[:, u % 2, i * P:(i + 1) * P],
                                            V[:, t, h * HV:(h + 1) * HV], start=i == 0, stop=i == len(keys) - 1)
                done(last)

            pe.wait_ge(sem("v"), TN)
            more = [(0, j) for j in range(8, 12)] + [(1, j) for j in range(12)]
            qk(0)
            score(0)
            score(1)
            for u in range(NU):
                if u % TN == 1 and u // TN + 1 < H:
                    qk(u // TN + 1)
                if u % TN == 3:
                    ada(*more.pop(0))
                if u + 2 < NU:
                    score(u + 2)
                ps = tile(("PT", u))
                pe.wait_ge(sem("p"), u + 1)
                for i in range(len(unit_keys(UNITS[u][1]))):
                    last = nc.tensor.transpose(ps[:, i * P:(i + 1) * P], Pr[:, u % 2, i * P:(i + 1) * P], ident[:, :])
                done(last)
                if u:
                    out(u - 1)
            out(NU - 1)
            for m in range(8):
                ps = tile(("OT", m))
                pe.wait_ge(sem("o"), NU)
                for t in range(TN):
                    last = nc.tensor.transpose(ps[:, t * P:(t + 1) * P], O[:, t, m * P:(m + 1) * P], ident[:, :])
                done(last)
            for m in range(8):
                tile(("l0", m))
                done(linear(("l0", m), Ahi, Alo, 0, SAT["attn"] + 1, BOTH))
            norm("n1")
            tile("r")
            done(linear("r", Ahi, Alo, 0, SAT["n1"] + 1, BOTH))
            for h in range(GH):
                tile(("gq", h))
                done(linear(("gq", h), Ahi, Alo, 0, None, XO))
                tile(("gk", h))
                done(linear(("gk", h), Ahi, Alo, 0, None, BOTH))
                for d, n in enumerate(["gf", "gb"]):
                    ps = tile((n, h))
                    pe.wait_ge(sem("gr"), 1)
                    pe.wait_ge(sem("glc"), 32)
                    for c0, c1 in BOTH:
                        last = nc.tensor.matmul(ps[:, c0:c1], wg[0:32, d, h * P:(h + 1) * P], gR[0:32, c0:c1],
                                                start=True, stop=True)
                    done(last)
                for t in range(2):
                    ps = tile(("gv", h, t))
                    for i in range(3):
                        for k in range(KD):
                            w = tuple(weights(("gv", h, t), 2 * k, GV))
                            tok = tuple(x[:, k, (3 * t + i) * P:(3 * t + i + 1) * P] for x in (Ahi, Alo))
                            last = product(ps[:, i * GV:(i + 1) * GV], tok, w, k == 0, k == KD - 1)
                    done(last)
                for m in range(2):
                    tile(("gg", h, m))
                    done(linear(("gg", h, m), Ahi, Alo, 0, None, XO))
                for l in range(8):
                    ps = tile(("lev", h, l))
                    if l == 0:
                        pe.wait_ge(sem("gq"), h + 1)
                        pe.wait_ge(sem("gk"), h + 1)
                        kk, qq = gk, gq
                    else:
                        pe.wait_ge(sem("lq"), 14 * h + 2 * l)
                        kk, qq = ex[:, l % 2, 1, :], ex[:, l % 2, 0, :]
                    for c in range(TX):
                        s = slice(c * P, (c + 1) * P)
                        last = nc.tensor.matmul(ps[:, s], kk[:, s], qq[:, s], start=True, stop=True)
                    done(last)
                for d in range(2):
                    ps = tile(("kT", h, d))
                    pe.wait_ge(sem("kd"), 2 * h + d + 1)
                    kdec = ex[:, d, :, :].rearrange("p a t -> p (a t)")
                    for t in range(TN):
                        last = nc.tensor.transpose(ps[:, t * P:(t + 1) * P], kdec[:, t * P:(t + 1) * P], ident[:, :])
                    done(last)
                    ps = tile(("st", h, d))
                    pe.wait_ge(sem("kT"), 2 * h + d + 1)
                    pe.wait_ge(sem("gv"), 2 * h + 2)
                    for i, ts in enumerate([[4, 5], [0], [1], [2]] if d == 0 else [[4, 5], [3], [2], [1]]):
                        for t in ts:
                            last = nc.tensor.matmul(ps[:, i * GV:(i + 1) * GV], kT[:, t * P:(t + 1) * P], gv[:, t, :],
                                                    start=t == ts[0], stop=t == ts[-1])
                    done(last)
                qd = ex[:, 0, :, :]
                for m in range(2):
                    ps = tile(("go", h, m))
                    pe.wait_ge(sem("qd"), 2 * h + 2)
                    pe.wait_ge(sem("st"), 8 * h + 8)
                    pe.wait_ge(sem("lev"), 15 * h + 15)
                    for c in range(TX):
                        s, f = slice(c * P, (c + 1) * P), slice(m * P, (m + 1) * P)
                        nc.tensor.matmul(ps[:, s], gv[:, c, f], At[:, s], start=True, stop=False)
                        nc.tensor.matmul(ps[:, s], S[:, 0, c, f], qd[:, 0, s], start=False, stop=False)
                        last = nc.tensor.matmul(ps[:, s], S[:, 1, c, f], qd[:, 1, s], start=False, stop=True)
                    done(last)
                norm(f"o{h}")
            for m in range(8):
                tile(("l1", m))
                done(linear(("l1", m), ghi, glo, 0, SAT["o0"] + 1, XO))
            norm("f1")
            norm("mix0")

            def s5_in(j):
                ps = tile(("sx", j))
                pe.wait_ge(sem("su"), j // 4 + 1)
                pe.wait_ge(sem("evc"), 16 * 5)
                r = slice(32 * (j % 4), 32 * (j % 4) + 32)
                for i in range(2):
                    last = nc.tensor.matmul(ps[:, i * T:(i + 1) * T], lB[r, j // 4, i, :], U[r, j // 4, :],
                                            start=True, stop=True)
                done(last)

            for m in range(2):
                tile(("su", m))
                done(linear(("su", m), Ahi, Alo, 0, SAT["mix0"] + 1, XO))
            for w in range(3):
                ps = tile(("mv", w))
                for t in range(TX):
                    for k in range(KD):
                        wt = tuple(weights(("mv", w), 2 * k, 2 * P))
                        tok = tuple(x[:, k, t * P:(t + 1) * P] for x in (Ahi, Alo))
                        last = product(ps[:, t * 256:(t + 1) * 256], tok, wt, k == 0, k == KD - 1)
                done(last)
                for j in range(2 * w, 2 * w + 2):
                    s5_in(j)
            for m in range(GM):
                tile(("mu", m))
                done(linear(("mu", m), Ahi, Alo, 0, None, XO))
                if m < 2:
                    s5_in(6 + m)
            for m in range(GM):
                ps = tile(("mg", m))
                pe.wait_ge(sem("mvn"), TX)
                pe.wait_ge(sem("gmw"), 1)
                for t in range(TX):
                    last = nc.tensor.matmul(ps[:, t * P:(t + 1) * P], mV[:, t, m * P:(m + 1) * P], gmw[:, m, :],
                                            start=True, stop=True)
                done(last)
            for c in range(2):
                ps = tile(("sy", c))
                pe.wait_ge(sem("lZ"), 2)
                for j in range(4 * c, 4 * c + 4):
                    pe.wait_ge(sem("sh"), j + 1)
                    r = slice(32 * (j % 4), 32 * (j % 4) + 32)
                    for i in range(2):
                        last = nc.tensor.matmul(ps[r, 0:T], lC[:, i, j, :], wS[:, j, i, :], start=i == 0, stop=i == 1)
                done(last)
            for c in range(2):
                ps = tile(("glu", c))
                pe.wait_ge(sem("y2"), 2)
                for k in range(2):
                    last = nc.tensor.matmul(ps[:, 0:T], glw[:, k, c * P:(c + 1) * P], U[:, k, :], start=k == 0, stop=k == 1)
                done(last)
            for m in range(8):
                tile(("ev", m))
                done(linear(("ev", m), Ahi, Alo, 0, SAT["gm"] + 1, XO, ks=EV_K))

            def ffn(l):
                norm(f"ffn{l}")
                for f in range(2):
                    for j in range(FH):
                        tile(("up", l, f, j))
                        for part in range(2):
                            last = linear(("up", l, f, j), Ahi, Alo, 0, SAT[f"ffn{l}"] + 1, XO, offset=KD * part,
                                          ks=list(range(KD)), col0=T * part)
                        done(last)
                    for m in range(8):
                        tile(("dn", l, f, m))
                        done(linear(("dn", l, f, m), Fhi, Flo, 0, SAT[f"act{l}{f}"] + 1, XO))

            ffn(0)
            norm("mix1")
            for m in range(8):
                tile(("ch", m))
                for part in range(2):
                    last = linear(("ch", m), Ahi, Alo, 0, SAT["mix1"] + 1, XO, offset=KD * part,
                                  ks=list(range(KD)), col0=T * part)
                done(last)
                tile(("bg", m))
                done(linear(("bg", m), Ahi, Alo, 0, None, XO))
            for m in range(8):
                tile(("od", m))
                done(linear(("od", m), Fhi, Flo, 0, SAT["od"] + 1, XO))
            ffn(1)
            norm("f2")
            assert at[0] == len(plan.free)

        @block.scalar
        def _(ac):
            for name in ("vec", "ident"):
                t = {"vec": vec, "ident": ident}[name]
                ac.dma_start(t[:, :], a[name]).then_inc(sem("consts"), 16)
            ac.dma_start(rope[:, :], a["rope"]).then_inc(sem("consts"), 16)
            ac.dma_start(eps1[:, :], a["eps1"]).then_inc(sem("consts"), 16)
            ac.dma_start(X[:, :, :], a["xT"]).then_inc(sem("xl"), 16)
            ac.dma_start(CX[:, :, :], a["ctxT"]).then_inc(sem("cl"), 16)
            nc.scalar.preload_act_table_set(LOG_EXP)
            do = Serial(ac, sem, "act")
            converted = [0]

            def psum(key):
                n = plan.index[key]
                while converted[0] < plan.nsplit:
                    s = converted[0]
                    if s >= CONV and plan.last[("split", s - CONV)] >= n:
                        break
                    c = plan.unit_at[("split", s)]
                    if plan.load_after[c] >= n:
                        break
                    if plan.first_use[s] > n + 6:
                        break
                    ac.wait_ge(sem(f"ld{c % RAW}"), 16 * (c // RAW + 1))
                    if s >= CONV:
                        ac.wait_ge(sem("psum"), plan.last[("split", s - CONV)] + 1)
                    nc.scalar.activation(whi[:, s % CONV, :], raw[:, c % RAW, :], ACT.Copy).then_inc(sem("whi"), 1)
                    converted[0] += 1
                ac.wait_ge(sem("psum"), n + 1)
                return PS[n % BANKS2]

            def act(out, in_, f, bias=None, scale=1.0, sem_name=None, accum=None):
                kw = {} if accum is None else {"accum_out": accum}
                if bias is not None:
                    kw["bias"] = bias
                do(nc.scalar.activation(out, in_, f, scale=scale, **kw), sem_name)

            def squares(name, tiles, waits):
                i = NI[name]
                for k in range(NORMS[i][1]):
                    g = NK[i] + k
                    if g >= 3:
                        g3 = g - 3
                        j = max(x for x in range(len(NORMS)) if NK[x] <= g3)
                        ac.wait_ge(sem("n_acc"), NA[j] + max(1, g3 - NK[j]))
                    for name_, value in waits(k):
                        ac.wait_ge(sem(name_), value)
                    for src, c0, c1 in tiles(k):
                        act(sq[:, g % 3, c0:c1], src, ACT.Square, sem_name="n_sq")

            def root(name):
                i = NI[name]
                _, _, width, n = NORMS[i]
                nc.scalar.preload_act_table_set(LOG_EXP)
                ps = psum(("ss", name))
                if i:
                    ac.wait_ge(sem("n_use"), i)
                act(rstd[:, 0:n], ps[:, 0:n], ACT.Ln, eps1[:, 0:1], 1.0 / width, "n_rs")
                act(rstd[:, 0:n], rstd[:, 0:n], ACT.Exp, None, -0.5, "n_rs")

            split = [0]

            def high(dst):
                ac.wait_ge(sem("hf"), split[0] + 1)
                act(dst, hf[:, split[0] % 2, 0:dst.shape[-1]], ACT.Copy, sem_name="hi")
                split[0] += 1

            ac.wait_ge(sem("consts"), 64)
            act(cnd[:, :], v_("cond", 0, 16), ACT.Silu, sem_name="cnd")
            nc.scalar.preload_act_table_set(LOG_EXP)
            ac.wait_ge(sem("xl"), 16)
            ac.wait_ge(sem("cl"), 16)
            both = lambda k: [(X[:, k, :], 0, T), (CX[:, k, :], T, N)]
            only = lambda k: [(X[:, k, :], 0, T)]
            squares("n0", both, lambda k: [])
            root("n0")
            for k in range(KD):
                high(Hhi[:, k, :])
            for m in range(5):
                ps = psum(("c", m))
                act(craw[:, m, :], ps[:, 0:N], ACT.Copy, sem_name="craw")
            squares("cq", lambda k: [(craw[:, k, :], 0, N)], lambda k: [])
            squares("ckv", lambda k: [(craw[:, 3 + k, :], 0, N)], lambda k: [])
            psum("kr")
            for m in range(8):
                ps = psum(("gate0", m))
                act(gate0[:, m, :], ps[:, 0:N], ACT.Silu, sem_name="gate0")
                if m in (1, 3):
                    nc.scalar.preload_act_table_set(LOG_EXP)
                if m == 1:
                    root("cq")
                    for k in range(3):
                        high(Chi[:, k, :])
                if m == 3:
                    root("ckv")
                    for k in range(2):
                        high(Chi[:, 3 + k, :])
            for t in range(TN):
                ps = psum(("v", t))
                act(V[:, t, :], ps[:, :], ACT.Copy, sem_name="v")
            nc.scalar.preload_act_table_set(LOG_EXP)
            sc = float(NOPE + ROPE) ** -0.5

            def qk(h):
                ps = psum(("Q", h))
                act(Q[0:64, h % 2, :], ps[0:64, 0:N], ACT.Copy, sem_name="q_nope")
                ps = psum(("K", h))
                act(K[0:64, h % 2, :], ps[0:64, 0:N], ACT.Copy, None, sc, "k_nope")

            def softmax(u):
                n = P * len(unit_keys(UNITS[u][1]))
                ps = psum(("S", u))
                if u >= 2:
                    ac.wait_ge(sem("psum"), plan.index[("PT", u - 2)] + 1)
                ac.wait_ge(sem("mx"), u + 1)
                act(Pr[:, u % 2, 0:n], ps[:, 0:n], ACT.Exp, small[:, 0, u % 8:u % 8 + 1], 1.0, "p",
                    small[:, 1, u % 8:u % 8 + 1])

            qk(0)
            softmax(0)
            softmax(1)
            for u in range(NU):
                if u % TN == 1 and u // TN + 1 < H:
                    qk(u // TN + 1)
                if u + 2 < NU:
                    softmax(u + 2)
            for m in range(8):
                psum(("OT", m))
                high(Ahi[:, m, :])
            for m in range(8):
                psum(("l0", m))
            squares("n1", both, lambda k: [("resid", k + 1), ("residc", k + 1)])
            ac.dma_start(wg[0:32, :, :], a["wg"]).then_inc(sem("glc"), 16)
            ac.dma_start(masks[:, :, :], a["masks"]).then_inc(sem("glc"), 16)
            root("n1")
            for k in range(KD):
                high(Ahi[:, k, :])
            ps = psum("r")
            act(gR[0:32, :], ps[0:32, 0:N], ACT.Copy, sem_name="gr")
            for h in range(GH):
                ps = psum(("gq", h))
                act(gq[:, :], ps[:, 0:T], ACT.Copy, None, float(GK) ** -0.5, "gq")
                ps = psum(("gk", h))
                act(gk[:, :], ps[:, 0:N], ACT.Copy, sem_name="gk")
                for d, n in enumerate(["gf", "gb"]):
                    ps = psum((n, h))
                    e = ex[:, d, :, :].rearrange("p a t -> p (a t)")[:, 0:N]
                    act(e, ps[:, 0:N], ACT.Abs, v_("b_" + n, h), 1.0, "g_log")
                    act(e, e, ACT.Exp, None, -1.0, "g_log")
                    act(e, e, ACT.Ln, eps1[:, 1:2], 1.0, "g_log")
                for t in range(2):
                    ps = psum(("gv", h, t))
                    act(gv[:, 3 * t:3 * t + 3, :], ps[:, 0:N].rearrange("p (i v) -> p i v", i=3), ACT.Copy, sem_name="gv")
                for m in range(2):
                    ps = psum(("gg", h, m))
                    act(gG[:, m, :], ps[:, 0:T], ACT.Silu, sem_name="gg")
                nc.scalar.preload_act_table_set(LOG_EXP)
                for l in range(1, 8):
                    ac.wait_ge(sem("le"), 28 * h + 4 * l)
                    act(ex[:, l % 2, :, :], ex[:, l % 2, :, :], ACT.Exp, None, 1.0 / GATE_NORM, "lx")
                ac.wait_ge(sem("edge"), 4 * h + 4)
                act(edge[:, 10:20], edge[:, 0:10], ACT.Exp, sem_name="kx")
                for d, (b, sign) in enumerate([(bF, -1.0), (nB, 1.0)]):
                    psum(("lev", h, 6 + d))
                    e = ex[:, d, :, :].rearrange("p a t -> p (a t)")
                    for c in range(5):
                        s = slice(c * P, (c + 1) * P) if c < 4 else slice(T, N)
                        act(e[:, s], b[:, s], ACT.Exp, edge[:, 5 * d + c:5 * d + c + 1], sign / GATE_NORM, "kx")
                ps = psum(("kT", h, 0))
                act(kT[:, :], ps[:, 0:N], ACT.Copy, sem_name="kT")
                act(ex[:, 0, 0, :], bF[:, 0:T], ACT.Exp, None, 1.0 / GATE_NORM, "qx")
                act(ex[:, 0, 1, :], nB[:, 0:T], ACT.Exp, None, -1.0 / GATE_NORM, "qx")
                ps = psum(("kT", h, 1))
                act(kT[:, :], ps[:, 0:N], ACT.Copy, sem_name="kT")
                for m in range(2):
                    ps = psum(("go", h, m))
                    act(ex[:, 1, m, :], ps[:, 0:T], ACT.Copy, sem_name="go")
                squares(f"o{h}", lambda k: [(ex[:, 1, k, :], 0, T)], lambda k: [])
                root(f"o{h}")
                for m in range(2):
                    high(ghi[:, 2 * h + m, :])
            for m in range(8):
                psum(("l1", m))
            squares("f1", only, lambda k: [("resid", RAT["l1"] + k + 1)])
            for t, n in [(lB, "lB"), (lC, "lC"), (glw, "glw"), (gmw, "gmw"), (bs, "bs")]:
                ac.dma_start(t[tuple([slice(None)] * len(t.shape))], a[n]).then_inc(sem("evc"), 16)
            root("f1")
            squares("mix0", only, lambda k: [("resid", RAT["f1"] + k + 1)])
            root("mix0")
            for k in range(KD):
                high(Ahi[:, k, 0:T])
            ac.wait_ge(sem("sp_a"), 1)
            act(sp[:, 1, :], v_("log_dt", 0, 8), ACT.Exp, sem_name="sp_b")
            ac.wait_ge(sem("sp_a"), 2)
            act(sp[:, 3, :], sp[:, 2, :], ACT.Exp, sem_name="sp_b")
            ac.wait_ge(sem("sp_a"), 3)
            act(sp[:, 7, :], sp[:, 6, :], ACT.Sin, sem_name="sp_b")
            act(sp[:, 8, :], sp[:, 9, :], ACT.Sin, sem_name="sp_b")
            nc.scalar.preload_act_table_set(LOG_EXP)
            for m in range(2):
                ps = psum(("su", m))
                act(U[:, m, :], ps[:, 0:T], ACT.Copy, sem_name="su")
            for w in range(3):
                ps = psum(("mv", w))
                act(mV[:, :, w * 256:(w + 1) * 256], ps[:, :].rearrange("p (t v) -> p t v", t=TX),
                    ACT.Gelu_apprx_tanh, sem_name="mv")
                for j in range(2 * w, 2 * w + 2):
                    psum(("sx", j))
            ac.wait_ge(sem("tab"), len(LEVELS))
            nc.scalar.preload_act_table_set(LOG_EXP)
            for t in range(TX):
                act(tmp[:, 0, 0:GM * P], mV[:, t, :], ACT.Square, None, 1.0, "mv_ss", mst[:, t:t + 1])
            act(mst[:, :], mst[:, :], ACT.Ln, eps1[:, 0:1], 1.0 / (GM * P), "mv_ss")
            act(mst[:, :], mst[:, :], ACT.Exp, None, -0.5, "mv_rs")
            for m in range(GM):
                ps = psum(("mu", m))
                act(mU[:, m, :], ps[:, 0:T], ACT.Gelu_apprx_tanh, sem_name="mu")
                if m < 2:
                    psum(("sx", 6 + m))
            for m in range(GM):
                psum(("mg", m))
                high(Ahi[:, 2 + m, 0:T])
            for c in range(2):
                psum(("sy", c))
                ac.wait_ge(sem("sy"), c + 1)
                act(U[:, c, :], U[:, c, :], ACT.Gelu_apprx_tanh, sem_name="y2")
            for c in range(2):
                ps = psum(("glu", c))
                act(tmp[:, 1, c * T:(c + 1) * T], ps[:, 0:T], ACT.Sigmoid, v_("b_glu", c), 1.0, "glu")
            for c in range(2):
                high(Ahi[:, c, 0:T])
            for m in range(8):
                psum(("ev", m))

            def ffn(l, before):
                squares(f"ffn{l}", only, lambda k: [("resid", RAT[before] + k + 1)])
                root(f"ffn{l}")
                for k in range(KD):
                    high(Ahi[:, k, 0:T])
                for f in range(2):
                    for r in range(FH + 2):
                        if r < FH:
                            ps = psum(("up", l, f, r))
                            j = (2 * l + f) * FH + r
                            if j >= 3:
                                ac.wait_ge(sem("hf"), hf_of(j - 3))
                            for part in range(2):
                                c = (part * 2 + f) * FH + r
                                act(cv[:, j % 3, part, :], ps[:, part * T:(part + 1) * T], ACT.Identity,
                                    v_(f"ffn_b{l}", c), v_(f"ffn_w{l}", 88 + c), "ca")
                        if 1 <= r <= FH:
                            j = (2 * l + f) * FH + r - 1
                            ac.wait_ge(sem("conv"), 4 * j + 4)
                            act(tmp[:, j % 2, 0:T], cv[:, j % 3, 0, :], ACT.Silu, sem_name="se")
                        if r >= 2:
                            high(Fhi[:, r - 2, :])
                    for m in range(8):
                        psum(("dn", l, f, m))

            ffn(0, "ev")
            squares("mix1", only, lambda k: [("resid", RAT["f01"] + k + 1)])
            root("mix1")
            for k in range(KD):
                high(Ahi[:, k, 0:T])
            for r in range(10):
                if r < 8:
                    ps = psum(("ch", r))
                    if r >= 3:
                        ac.wait_ge(sem("hf"), SAT["od"] + r - 2)
                    act(cv[:, r % 3, 0, :], ps[:, 0:T], ACT.Copy, sem_name="oc")
                if 1 <= r <= 8:
                    m = r - 1
                    ac.wait_ge(sem("ch"), m + 1)
                    act(tmp[:, m % 2, 0:T], cv[:, m % 3, 1, :], ACT.Identity, v_("od_b", m), v_("od_w", 16 + m), "oa")
                if r >= 2:
                    high(Fhi[:, r - 2, :])
            for m in range(8):
                psum(("od", m))
            ffn(1, "od")
            squares("f2", only, lambda k: [("resid", RAT["f11"] + k + 1)])
            root("f2")

        @block.vector
        def _(ve):
            do = Serial(ve, sem, "dve")
            TTi, TSi, STTi = nc.vector.tensor_tensor, nc.vector.tensor_scalar, nc.vector.scalar_tensor_tensor

            def tt(out, x, y, op, s=None):
                do(TTi(out, x, y, op), s)

            def ts(out, x, s1, s2, op0, op1=None, s=None):
                do(TSi(out, x, s1, s2, op0, op1) if op1 is not None else TSi(out, x, s1, None, op0), s)

            def stt(out, x, sc, y, op0, op1, s=None):
                do(STTi(out, x, sc, y, op0, op1), s)

            def psum(key):
                ve.wait_ge(sem("psum"), plan.index[key] + 1)
                return PS[plan.index[key] % BANKS2]

            ADD, SUB, MUL, MAX, MIN = ALU.add, ALU.subtract, ALU.mult, ALU.max, ALU.min
            nsq = [0]

            def sums(name):
                i = NI[name]
                _, k_, _, n = NORMS[i]
                per = 2 if name in ("n0", "n1") else 1
                if i:
                    ve.wait_ge(sem("psum"), plan.index[("ss", NORMS[i - 1][0])] + 1)
                for k in range(1, k_):
                    ve.wait_ge(sem("n_sq"), nsq[0] + per * (k + 1))
                    g = NK[i] + k
                    first = sq[:, (g - 1) % 3, 0:n] if k == 1 else acc[:, 0:n]
                    tt(acc[:, 0:n], first, sq[:, g % 3, 0:n], ADD, "n_acc")
                nsq[0] += per * k_

            made, waiting = [0], []

            def low():
                dst, i = waiting.pop(0)
                hi, lo = dst
                ve.wait_ge(sem("hi"), i + 1)
                tt(lo, hf[:, i % 2, 0:lo.shape[-1]], hi.bitcast(fp32), SUB, "lo")

            def to_split(n):
                if len(waiting) == 2:
                    low()
                return hf[:, made[0] % 2, 0:n]

            def queued(hi, lo):
                waiting.append(((hi, lo), made[0]))
                made[0] += 1

            def flush():
                while waiting:
                    low()

            def apply(name, src, gain, hi, lo, n, extra=None):
                i = NI[name]
                ve.wait_ge(sem("n_rs"), 2 * i + 2)
                for k in range(NORMS[i][1]):
                    b = to_split(n)
                    if extra is None:
                        stt(b, src(k), gain(k), rstd[:, 0:n], MUL, MUL, "hf")
                    else:
                        stt(b, src(k), gain(k), rstd[:, 0:n], MUL, MUL)
                        tt(b, b, extra(k), MUL, "hf")
                    queued(hi(k), lo(k))
                flush()
                ts(small2[:, 0:1], eps1[:, 0:1], 1.0, None, MUL, s="n_use")

            def modulated(name, layer, hi, lo):
                i = NI[name]
                ve.wait_ge(sem("n_rs"), 2 * i + 2)
                for k in range(KD):
                    b = to_split(N)
                    for c, (src, s) in enumerate([(X, slice(0, T)), (CX, slice(T, N))]):
                        tt(b[:, s], src[:, k, :], rstd[:, s], MUL)
                        ts(b[:, s], b[:, s], sc1[:, layer, 2 * k + c:2 * k + c + 1], mod[:, layer, 2 * k + c:2 * k + c + 1],
                           MUL, ADD, s="hf" if c else None)
                    queued(hi[:, k, :], lo[:, k, :])
                flush()
                ts(small2[:, 0:1], eps1[:, 0:1], 1.0, None, MUL, s="n_use")

            def ada(layer, j):
                ps = psum(("ada", layer, j))
                tt(mod[:, layer, 4 * j:4 * j + 4], ps[:, 0:4], v_(f"ada_b{layer}", 4 * j, 4), ADD, "mod")

            def scales(layer):
                stt(sc1[:, layer, :], mod[:, layer, 16:32], 1.0, v_(f"norm_g{layer}", 0, 16), ADD, MUL)

            do(nc.vector.memset(ones[:, :], 1.0), "ones")
            do(nc.vector.memset(small2[:, :], 0.0), "ones")
            ve.wait_ge(sem("consts"), 64)
            sums("n0")
            for j in range(8):
                ada(0, j)
            scales(0)
            modulated("n0", 0, Hhi, Hlo)
            ve.wait_ge(sem("craw"), 5)
            sums("cq")
            ps = psum("kr")
            r, r2 = slice(64, 96), slice(96, 128)
            sc = float(NOPE + ROPE) ** -0.5
            tt(K[r, 0, 0:T], ps[r, 0:T], rope[r, :], MUL, "kr")
            tt(PT[r, 1, 0:T], ps[r2, 0:T], rope[r2, :], MUL, "kr")
            tt(K[r, 0, 0:T], K[r, 0, 0:T], PT[r, 1, 0:T], ADD, "kr")
            do(nc.vector.tensor_copy(K[r, 0, T:N], ps[r, T:N]), "kr")
            ts(K[r, 0, :], K[r, 0, :], sc, None, MUL, s="kr")
            do(nc.vector.tensor_copy(K[r, 1, :], K[r, 0, :]), "kr")
            apply("cq", lambda k: craw[:, k, :], lambda k: v_("q_g", k), lambda k: Chi[:, k, :],
                  lambda k: Clo[:, k, :], N)
            sums("ckv")
            apply("ckv", lambda k: craw[:, 3 + k, :], lambda k: v_("kv_g", k), lambda k: Chi[:, 3 + k, :],
                  lambda k: Clo[:, 3 + k, :], N)

            def q_rope(h):
                ps = psum(("Q", h))
                ve.wait_ge(sem("q_nope"), h + 1)
                tt(Q[r, h % 2, 0:T], ps[r, 0:T], rope[r, :], MUL, "q_rope")
                tt(acc[r, 0:T], ps[r2, 0:T], rope[r2, :], MUL, "q_rope")
                tt(Q[r, h % 2, 0:T], Q[r, h % 2, 0:T], acc[r, 0:T], ADD, "q_rope")
                do(nc.vector.tensor_copy(Q[r, h % 2, T:N], ps[r, T:N]), "q_rope")

            def row_max(u):
                n = P * len(unit_keys(UNITS[u][1]))
                ps = psum(("S", u))
                do(nc.vector.tensor_reduce(small[:, 0, u % 8:u % 8 + 1], ps[:, 0:n], AX.X, MAX, negate=True), "mx")

            def out(u):
                h, q = UNITS[u]
                ve.wait_ge(sem("p"), u + 1)
                do(nc.vector.reciprocal(small[:, 2, u % 8:u % 8 + 1], small[:, 1, u % 8:u % 8 + 1]))
                ps = psum(("O", u))
                ts(O[:, q, h * HV:(h + 1) * HV], ps[:, 0:HV], small[:, 2, u % 8:u % 8 + 1], None, MUL, s="o")

            more = [(0, j) for j in range(8, 12)] + [(1, j) for j in range(12)]
            q_rope(0)
            row_max(0)
            row_max(1)
            for u in range(NU):
                if u % TN == 1 and u // TN + 1 < H:
                    q_rope(u // TN + 1)
                if u % TN == 3:
                    ada(*more.pop(0))
                if u + 2 < NU:
                    row_max(u + 2)
                n = P * len(unit_keys(UNITS[u][1]))
                ps = psum(("PT", u))
                do(nc.vector.tensor_copy(PT[:, u % 2, 0:n], ps[:, 0:n]), "pt")
                if u:
                    out(u - 1)
            out(NU - 1)
            scales(1)
            for m in range(8):
                ps = psum(("OT", m))
                b = to_split(N)
                ve.wait_ge(sem("gate0"), m + 1)
                tt(b, ps[:, 0:N], gate0[:, m, :], MUL, "hf")
                queued(Ahi[:, m, :], Alo[:, m, :])
            flush()

            def resid(key, m, gate=None, n_sem="resid"):
                ps = psum(key)
                if gate is None:
                    tt(X[:, m, :], ps[:, 0:T], X[:, m, :], ADD, n_sem)
                else:
                    stt(X[:, m, :], ps[:, 0:T], gate, X[:, m, :], MUL, ADD, n_sem)

            for m in range(8):
                resid(("l0", m), m, mod[:, 0, 32 + 2 * m:33 + 2 * m])
                ps = psum(("l0", m))
                stt(CX[:, m, :], ps[:, T:N], mod[:, 0, 33 + 2 * m:34 + 2 * m], CX[:, m, :], MUL, ADD, "residc")
            sums("n1")
            modulated("n1", 1, Ahi, Alo)
            for h in range(GH):
                for d, n in enumerate(["gf", "gb"]):
                    ps = psum((n, h))
                    b = (bF, nB)[d]
                    ve.wait_ge(sem("g_log"), 6 * h + 3 * d + 1)
                    ts(b[:, :], ps[:, 0:N], v_("b_" + n, h), 0.0, ADD, MIN, s="g_min")
                    ve.wait_ge(sem("g_log"), 6 * h + 3 * d + 3)
                    tt(b[:, :], b[:, :], ex[:, d, :, :].rearrange("p a t -> p (a t)")[:, 0:N], SUB)
                    pre = ex[:, 0, :, :].rearrange("p a t -> p (a t)")
                    for c in range(5):
                        s = slice(c * P, (c + 1) * P) if c < 4 else slice(T, N)
                        w = s.stop - s.start
                        if d == 0:
                            do(nc.vector.tensor_tensor_scan(b[:, s], ones[:, 0:w], b[:, s], 0.0, MUL, ADD))
                        else:
                            do(nc.vector.tensor_tensor_scan(pre[:, s], ones[:, 0:w], b[:, s], 0.0, MUL, ADD))
                            stt(b[:, s], pre[:, s], pre[:, s.stop - 1:s.stop], b[:, s], SUB, SUB)
                ve.wait_ge(sem("kx"), 11 * h) if h else None
                k16 = 1.0 / GATE_NORM
                bx, nx = bF[:, 0:T].rearrange("p (c t) -> p c t", c=4), nB[:, 0:T].rearrange("p (c t) -> p c t", c=4)
                ts(edge[:, 0:4], bx[:, :, P - 1], k16, None, MUL, s="edge")
                ts(edge[:, 4:5], bF[:, N - 1:N], k16, None, MUL, s="edge")
                ts(edge[:, 5:9], nx[:, :, 0], -k16, None, MUL, s="edge")
                ts(edge[:, 9:10], nB[:, T:T + 1], -k16, None, MUL, s="edge")

                def exponents(l):
                    b = LEVELS[l - 1]
                    f, n_ = (x[:, 0:T].rearrange("p (n s b) -> p n s b", s=2, b=b) for x in (bF, nB))
                    eq, ek = (ex[:, l % 2, i, :].rearrange("p (n s b) -> p n s b", s=2, b=b) for i in range(2))
                    shape = [P, T // (2 * b), b]
                    fm = f[:, :, 0, b - 1:b].to_broadcast(shape)
                    nm = n_[:, :, 1, 0:1].to_broadcast(shape)
                    tt(eq[:, :, 1, :], f[:, :, 1, :], fm, SUB, "le")
                    tt(ek[:, :, 0, :], fm, f[:, :, 0, :], SUB, "le")
                    tt(eq[:, :, 0, :], nm, n_[:, :, 0, :], SUB, "le")
                    tt(ek[:, :, 1, :], n_[:, :, 1, :], nm, SUB, "le")

                def masked(l):
                    ps = psum(("lev", h, l))
                    m = masks[:, l:l + 1, :].to_broadcast([P, 4, P])
                    src = ps[:, 0:T].rearrange("p (c t) -> p c t", c=4)
                    dst = (Am if l else At)[:, :].rearrange("p (c t) -> p c t", c=4)
                    tt(dst, src, m, MUL, "lev")
                    if l:
                        tt(At[:, :], At[:, :], Am[:, :], ADD, "lev")

                ve.wait_ge(sem("glc"), 32)
                exponents(1)
                masked(0)
                ve.wait_ge(sem("gk"), h + 1)
                ve.wait_ge(sem("gg"), 2 * h + 2)
                for l in range(1, 8):
                    ve.wait_ge(sem("lx"), 7 * h + l)
                    tt(ex[:, l % 2, 0, :], ex[:, l % 2, 0, :], gq[:, :], MUL, "lq")
                    tt(ex[:, l % 2, 1, :], ex[:, l % 2, 1, :], gk[:, 0:T], MUL, "lq")
                    if l >= 2:
                        masked(l - 1)
                    if l < 7:
                        exponents(l + 1)
                masked(7)
                for d in range(2):
                    ve.wait_ge(sem("kx"), 11 * h + 6 + 5 * d)
                    e = ex[:, d, :, :].rearrange("p a t -> p (a t)")
                    tt(e[:, 0:N], e[:, 0:N], gk[:, :], MUL, "kd")
                for i in range(2):
                    if i == 0:
                        ps = psum(("st", h, 0))
                        do(nc.vector.tensor_copy(S[:, 0, 0, :], ps[:, 0:GV]), "st")
                        for c in range(3):
                            stt(S[:, 0, c + 1, :], S[:, 0, c, :], edge[:, 10 + c:11 + c], ps[:, (c + 1) * GV:(c + 2) * GV],
                                MUL, ADD, "st")
                        for j in range(2):
                            ve.wait_ge(sem("qx"), 2 * h + j + 1)
                            tt(ex[:, 0, j, :], ex[:, 0, j, :], gq[:, :], MUL, "qd")
                    else:
                        ps = psum(("st", h, 1))
                        do(nc.vector.tensor_copy(S[:, 1, 3, :], ps[:, 0:GV]), "st")
                        for n, c in enumerate([3, 2, 1]):
                            stt(S[:, 1, c - 1, :], S[:, 1, c, :], edge[:, 15 + c:16 + c], ps[:, (n + 1) * GV:(n + 2) * GV],
                                MUL, ADD, "st")
                sums(f"o{h}")
                apply(f"o{h}", lambda k: ex[:, 1, k, :], lambda k: v_("o_g", k), lambda k: ghi[:, 2 * h + k, :],
                      lambda k: glo[:, 2 * h + k, :], T, lambda k: gG[:, k, :])
            for m in range(8):
                resid(("l1", m), m, mod[:, 1, 32 + 2 * m:33 + 2 * m])
            sums("f1")
            ve.wait_ge(sem("n_rs"), 2 * NI["f1"] + 2)
            for k in range(KD):
                stt(X[:, k, :], X[:, k, :], v_("final_g", k), rstd[:, 0:T], MUL, MUL, "resid")
            ts(small2[:, 0:1], eps1[:, 0:1], 1.0, None, MUL, s="n_use")
            sums("mix0")
            apply("mix0", lambda k: X[:, k, :], lambda k: v_("mix_g0", k), lambda k: Ahi[:, k, 0:T],
                  lambda k: Alo[:, k, 0:T], T)

            def col(i):
                return sp[:, i, :]

            ve.wait_ge(sem("evc"), 16 * 5)
            lr, li = col(0), v_("lam_im", 0, 8)
            ts(lr, v_("lam_re", 0, 8), -1e-4, None, MIN, s="sp_a")
            ve.wait_ge(sem("sp_b"), 1)
            tt(col(4), li, col(1), MUL)
            tt(col(2), lr, col(1), MUL, "sp_a")
            big = 1.5 * 2.0 ** 23
            ts(col(5), col(4), float(1.0 / (2.0 * np.pi)), big, MUL, ADD)
            ts(col(5), col(5), big, None, SUB)
            c1, c2 = 6.28125, float(np.float32(2.0 * np.pi - 6.28125))
            c3 = float(2.0 * np.pi - 6.28125 - c2)
            stt(col(6), col(5), -c1, col(4), MUL, ADD)
            stt(col(6), col(5), -c2, col(6), MUL, ADD)
            stt(col(6), col(5), -c3, col(6), MUL, ADD)
            pi = 3.1415925
            ts(col(6), col(6), pi, -pi, MIN, MAX)
            ts(col(9), col(6), 0.5, None, MUL, s="sp_a")
            ve.wait_ge(sem("sp_b"), 4)
            tt(col(10), col(8), col(8), MUL)
            ts(col(10), col(10), -2.0, 1.0, MUL, ADD)
            tt(col(11), col(3), col(10), MUL)
            ts(col(11), col(11), -1.0, None, ADD)
            tt(col(12), col(3), col(7), MUL)
            tt(col(13), lr, lr, MUL)
            tt(col(14), li, li, MUL)
            tt(col(13), col(13), col(14), ADD)
            do(nc.vector.reciprocal(col(13), col(13)))
            tt(col(15), col(11), lr, MUL)
            tt(col(16), col(12), li, MUL)
            tt(col(15), col(15), col(16), ADD)
            tt(col(15), col(15), col(13), MUL)
            tt(col(16), col(12), lr, MUL)
            tt(col(17), col(11), li, MUL)
            tt(col(16), col(16), col(17), SUB)
            tt(col(16), col(16), col(13), MUL)
            zr, zi = (sp[:, i, :].rearrange("p (g o) -> p g o", o=1).to_broadcast([P, SG, 32]) for i in (15, 16))
            t0, t1, t2 = (tmp[:, 0, i * 256:(i + 1) * 256].rearrange("p (g o) -> p g o", o=32) for i in range(3))
            tt(t0, lC[:, 0, :, :], zr, MUL)
            tt(t1, lC[:, 1, :, :], zi, MUL)
            tt(t0, t0, t1, SUB)
            tt(t1, lC[:, 0, :, :], zi, MUL)
            tt(t2, lC[:, 1, :, :], zr, MUL)
            do(nc.vector.tensor_copy(lC[:, 0, :, :], t0), "lZ")
            stt(lC[:, 1, :, :], t1, -1.0, t2, MUL, SUB, "lZ")
            do(nc.vector.tensor_copy(tab[:, 0, :, 0], col(10)))
            do(nc.vector.tensor_copy(tab[:, 1, :, 0], col(7)))
            for b in LEVELS:
                shape = [P, SG, b]
                cm, sm = (tab[:, i, :, b - 1:b].to_broadcast(shape) for i in range(2))
                cs, sn = (tab[:, i, :, 0:b] for i in range(2))
                t0, t1 = (tmp[:, 0, i * 512:i * 512 + SG * b].rearrange("p (g o) -> p g o", g=SG) for i in range(2))
                tt(t0, cs, cm, MUL)
                tt(t1, sn, sm, MUL)
                tt(tab[:, 0, :, b:2 * b], t0, t1, SUB)
                tt(t0, cs, sm, MUL)
                tt(t1, sn, cm, MUL)
                tt(tab[:, 1, :, b:2 * b], t0, t1, ADD, "tab")
            def rotate(x, j, back):
                cs, sn = (tab[:, i, j:j + 1, :].to_broadcast([P, 8, P]) for i in range(2))
                a_, b_ = tmp[:, 1, :], wtmp
                v8 = lambda y: y.rearrange("p (c t) -> p c t", c=8)
                tt(v8(a_), v8(x), cs, MUL)
                tt(v8(b_), v8(x), sn, MUL, None if back else "sx")
                re, im = wS[:, j, 0, :], wS[:, j, 1, :]
                tt(re, a_[:, 0:T], b_[:, T:2 * T], SUB if back else ADD)
                tt(im, a_[:, T:2 * T], b_[:, 0:T], ADD if back else SUB, "sh" if back else None)

            for w in range(3):
                for j in range(2 * w, 2 * w + 2):
                    rotate(psum(("sx", j))[:, :], j, False)
            ve.wait_ge(sem("mv_rs"), 1)
            for t in range(TX):
                ts(mV[:, t, :], mV[:, t, :], mst[:, t:t + 1], None, MUL, s="mvn")
            for j in (6, 7):
                rotate(psum(("sx", j))[:, :], j, False)
            for m in range(GM):
                ps = psum(("mg", m))
                v4 = lambda y: y.rearrange("p (c t) -> p c t", c=4)
                stt(v4(tmp[:, 1, 0:T]), v4(ps[:, 0:T]), v_("v_g", m), bs[:, m:m + 1, :].to_broadcast([P, 4, P]), MUL, ADD, "mg")
                ve.wait_ge(sem("mu"), m + 1)
                b = to_split(T)
                tt(b, tmp[:, 1, 0:T], mU[:, m, :], MUL, "hf")
                queued(Ahi[:, 2 + m, 0:T], Alo[:, 2 + m, 0:T])
            flush()
            for c in range(4):
                for j in range(SG):
                    for i in range(2):
                        s = wS[:, j, i, c * P:(c + 1) * P]
                        init = 0.0 if c == 0 else sp[:, 24 + i, j:j + 1]
                        do(nc.vector.tensor_tensor_scan(s, sp[:, 3, j:j + 1].to_broadcast([P, P]), s, init, MUL, ADD))
                if c < 3:
                    gr, gi = (wS[:, :, i, c * P + P - 1] for i in range(2))
                    ct, st_ = (tab[:, i, :, P - 1] for i in range(2))
                    tt(col(26), gr, ct, MUL)
                    tt(col(27), gi, st_, MUL)
                    tt(col(24), col(26), col(27), SUB)
                    tt(col(26), gi, ct, MUL)
                    tt(col(27), gr, st_, MUL)
                    tt(col(25), col(26), col(27), ADD)
            for j in range(SG):
                rotate(wS[:, j, :, :].rearrange("p i t -> p (i t)"), j, True)
            for c in range(2):
                ps = psum(("sy", c))
                stt(U[:, c, :], U[:, c, :], v_("s5_d", c), ps[:, 0:T], MUL, ADD, "sy")
            for c in range(2):
                ve.wait_ge(sem("glu"), c + 1)
                e = tmp[:, 1, c * T:(c + 1) * T]
                b = to_split(T)
                tt(b, e, U[:, c, :], MUL, "hf")
                queued(Ahi[:, c, 0:T], Alo[:, c, 0:T])
            flush()
            for m in range(8):
                resid(("ev", m), m)

            def ffn(l):
                sums(f"ffn{l}")
                apply(f"ffn{l}", lambda k: X[:, k, :], lambda k: v_(f"ffn_g{l}", k), lambda k: Ahi[:, k, 0:T],
                      lambda k: Alo[:, k, 0:T], T)
                for f in range(2):
                    for r_ in range(FH + 1):
                        if r_ < FH:
                            ps = psum(("up", l, f, r_))
                            j = (2 * l + f) * FH + r_
                            for part in range(2):
                                ve.wait_ge(sem("ca"), 2 * j + part + 1)
                                c = (part * 2 + f) * FH + r_
                                for back in (1, 2):
                                    y = cv[:, j % 3, part, back:T]
                                    stt(y, ps[:, part * T:part * T + T - back], v_(f"ffn_w{l}", 44 * (2 - back) + c), y,
                                        MUL, ADD, "conv")
                        if r_:
                            j = (2 * l + f) * FH + r_ - 1
                            ve.wait_ge(sem("se"), j + 1)
                            e = tmp[:, j % 2, 0:T]
                            b = to_split(T)
                            tt(b, e, cv[:, j % 3, 1, :], MUL, "hf")
                            queued(Fhi[:, r_ - 1, :], Flo[:, r_ - 1, :])
                    flush()
                    for m in range(8):
                        resid(("dn", l, f, m), m)

            ffn(0)
            sums("mix1")
            apply("mix1", lambda k: X[:, k, :], lambda k: v_("mix_g1", k), lambda k: Ahi[:, k, 0:T],
                  lambda k: Alo[:, k, 0:T], T)
            for r_ in range(9):
                if r_ < 8:
                    ps = psum(("ch", r_))
                    ve.wait_ge(sem("oc"), r_ + 1)
                    tt(cv[:, r_ % 3, 1, :], cv[:, r_ % 3, 0, :], ps[:, T:2 * T], MUL, "ch")
                if r_:
                    m = r_ - 1
                    ve.wait_ge(sem("oa"), m + 1)
                    ps = psum(("bg", m))
                    for back in (1, 2):
                        y = tmp[:, m % 2, back:T]
                        stt(y, cv[:, m % 3, 1, 0:T - back], v_("od_w", 8 * (2 - back) + m), y, MUL, ADD)
                    b = to_split(T)
                    tt(b, tmp[:, m % 2, 0:T], ps[:, 0:T], MUL, "hf")
                    queued(Fhi[:, m, :], Flo[:, m, :])
            flush()
            for m in range(8):
                resid(("od", m), m)
            ffn(1)
            sums("f2")
            ve.wait_ge(sem("n_rs"), 2 * NI["f2"] + 2)
            for k in range(KD):
                stt(X[:, k, :], X[:, k, :], v_("final_g2", k), rstd[:, 0:T], MUL, MUL, "out")


def _swap(w):
    return np.concatenate([w[..., 8:16], w[..., 0:8], w[..., 24:32], w[..., 16:24]], -1)


def _matrices(w):
    z = lambda *s: np.zeros(s, np.float32)
    m = {}
    wi = w["mla_w_in"][0]
    kr = wi[:, QR + KVR:QR + KVR + ROPE]
    m["win0"] = np.concatenate([wi[:, :QR + KVR], z(D, 64), kr, _swap(kr), wi[:, QR + KVR + ROPE:]], 1)
    uq = w["mla_w_uq"][0].reshape(QR, H, NOPE + ROPE)
    m["uq"] = np.concatenate([uq, _swap(uq[..., NOPE:])], -1).reshape(QR, H * P)
    ukv = w["mla_w_ukv"][0].reshape(KVR, H, NOPE + HV)
    m["uk"] = np.concatenate([ukv[..., :NOPE], z(KVR, H, P - NOPE)], -1).reshape(KVR, H * P)
    m["uv"] = ukv[..., NOPE:].reshape(KVR, H * HV)
    m["wout0"], m["wout1"] = w["mla_w_out"][0], w["gla_w_out"][0]
    gi = w["gla_w_in"][0]
    m["gin"] = gi[:, :3 * D]
    m["gr"] = np.concatenate([gi[:, 3 * D:], z(D, P - 32)], 1)
    m["ein"], m["eout"] = w["ev_w_in_2"][0], w["ev_w_out_2"][0]
    m["oin"], m["oout"] = w["od_w_in_2"][0], w["od_w_out_2"][0]
    for l in range(2):
        m[f"up{l}"], m[f"dn{l}"] = w["ffn_w_up_2"][l], w["ffn_w_down_2"][l]
    return m


def _columns(v):
    return np.asarray(v).reshape(-1, P).T


def _arrays(w):
    w = {k: np.asarray(v) for k, v in w.items()}
    mats = _matrices(w)
    units = np.zeros((len(PLAN.units), P, UT, P), np.float32)
    for c, (kind, i) in enumerate(PLAN.units):
        for j in range(UT):
            if kind == "raw":
                units[c, :, j, :] = w["ada_w"][i // 24][j * P:(j + 1) * P, i % 24 * P:(i % 24 + 1) * P]
            elif i * UT + j < len(PLAN.split):
                name, k, m = PLAN.split[i * UT + j]
                units[c, :, j, :] = mats[name][k * P:(k + 1) * P, m * P:(m + 1) * P]
    twice = lambda v: np.repeat(_columns(v), 2, 1)
    parts = {
        "cond": np.stack([_columns(w["c"][0]), _columns(w["c_ctx"])], 2).reshape(P, 16),
        "ada_b0": twice(w["ada_b"][0]), "ada_b1": twice(w["ada_b"][1]),
        "norm_g0": twice(w["norm_g"][0]), "norm_g1": twice(w["norm_g"][1]),
        "final_g": _columns(w["final_g"]), "q_g": _columns(w["mla_q_norm"][0]),
        "kv_g": _columns(w["mla_kv_norm"][0]), "b_gf": _columns(w["gla_b_gf"][0]),
        "b_gb": _columns(w["gla_b_gb"][0]), "o_g": _columns(w["gla_o_norm"][0]),
        "mix_g0": _columns(w["mix_norm_g_2"][0]), "mix_g1": _columns(w["mix_norm_g_2"][1]),
        "ffn_g0": _columns(w["ffn_norm_g_2"][0]), "ffn_g1": _columns(w["ffn_norm_g_2"][1]),
        "final_g2": _columns(w["final_norm_g_2"]),
        "lam_re": _columns(w["s5_lam_re_2"][0]), "lam_im": _columns(w["s5_lam_im_2"][0]),
        "log_dt": _columns(np.repeat(w["s5_log_dt_2"][0], 64)),
        "s5_d": _columns(w["s5_d_2"][0]), "b_glu": _columns(w["s5_b_glu_2"][0]),
        "v_g": _columns(w["gm_v_g_2"][0]), "od_w": _columns(w["od_conv_w_2"][0]),
        "od_b": _columns(w["od_conv_b_2"][0]),
        "ffn_w0": _columns(w["ffn_conv_w_2"][0]), "ffn_w1": _columns(w["ffn_conv_w_2"][1]),
        "ffn_b0": _columns(w["ffn_conv_b_2"][0]), "ffn_b1": _columns(w["ffn_conv_b_2"][1]),
    }
    vec = np.concatenate([parts[n] for n, _ in VECS], 1)
    assert vec.shape == (P, NV)
    t = np.arange(T)
    inv = np.float32(10000.0) ** (-np.arange(8, dtype=np.float32) / np.float32(8))
    ang = [(pos.astype(np.float32)[None, :] * inv[:, None]).astype(np.float32) for pos in (t // 64, t % 64)]
    cos, sin = [np.cos(x) for x in ang], [np.sin(x) for x in ang]
    rope = np.zeros((P, T), np.float32)
    rope[64:96] = np.concatenate([cos[0], cos[0], cos[1], cos[1]])
    rope[96:128] = np.concatenate([-sin[0], sin[0], -sin[1], sin[1]])
    wg = np.zeros((32, 2, 512), np.float32)
    wg[0:16, 0], wg[16:32, 1] = w["gla_w_gf"][0], w["gla_w_gb"][0]
    i = np.arange(P)
    masks = np.zeros((P, 8, P), np.float32)
    masks[:, 0] = 2.0 * (i[:, None] == i[None, :])
    for l, b in enumerate(LEVELS):
        masks[:, l + 1] = (i[:, None] // (2 * b) == i[None, :] // (2 * b)) & (i[:, None] // b != i[None, :] // b)
    lB, lC = np.zeros((P, 2, 2, P), np.float32), np.zeros((P, 2, SG, 32), np.float32)
    for j in range(SG):
        for g in range(2):
            for r, (b, c) in enumerate([("s5_b_re_2", "s5_c_re_2"), ("s5_b_im_2", "s5_c_im_2")]):
                at = 32 * (j % 4) + 16 * g
                lB[at:at + 16, j // 4, r, 64 * g:64 * g + 64] = w[b][0, 2 * j + g].T
                lC[64 * g:64 * g + 64, r, j, 16 * g:16 * g + 16] = w[c][0, 2 * j + g].T
    eps1 = np.zeros((P, 2), np.float32)
    eps1[:, 0], eps1[:, 1] = EPS, 1.0
    return {
        "units": units.reshape(len(PLAN.units), P, UT * P), "vec": vec, "rope": rope, "eps1": eps1,
        "ident": np.eye(P, dtype=np.float32), "wg": wg, "masks": masks, "lB": lB, "lC": lC,
        "xT": w["x"][0].T.reshape(KD, P, T).transpose(1, 0, 2),
        "ctxT": w["ctx"][0].T.reshape(KD, P, TC).transpose(1, 0, 2),
        "glw": w["s5_w_glu_2"][0].reshape(2, P, SW).transpose(1, 0, 2),
        "gmw": w["gm_w_s_2"][0].transpose(2, 0, 1),
        "bs": np.broadcast_to(w["gm_b_s_2"][0][None], (P, GM, P)),
    }


def kernel(**inputs):
    import concourse.bacc as bacc
    from concourse.bass_utils import run_bass_kernel_spmd

    nc = bacc.Bacc("TRN2", target_bir_lowering=False, num_devices=1, dynamic_dma_scratch_size=64)
    arrays = {f"in_{k}": np.ascontiguousarray(v) for k, v in _arrays(inputs).items()}
    a = {k[3:]: nc.dram_tensor(k, v.shape, mybir.dt.float32, kind="ExternalInput").ap() for k, v in arrays.items()}
    a["out"] = nc.dram_tensor("out_xT", (P, KD, T), mybir.dt.float32, kind="ExternalOutput").ap()
    build(nc, a)
    r = run_bass_kernel_spmd(nc, [arrays], core_ids=[0])
    got = r.results[0]["out_xT"]
    return got.transpose(1, 0, 2).reshape(D, T).T[None]
```

```python
from contextlib import ExitStack

import numpy as np

import concourse.bass as bass
from concourse import mybir

D, T, TC = 1024, 512, 256
N = T + TC
P = 128
KD = D // P
TX, TCX, TN = T // P, TC // P, N // P
H, NOPE, ROPE, HV = 16, 64, 32, 64
QR, KVR = 384, 256
GH, GK, GV = 4, 128, 256
GATE_NORM = 16.0
LEVELS = [1, 2, 4, 8, 16, 32, 64]
SG = 8
SW = D // 4
GM = 6
DFF = 2816
FH = DFF // P // 2
EPS = 1e-6
UT = 8
RAW, CONV = 5, 3
AHEAD = 7
EAGER = ("up", "ch", "dn", "od")
BANKS2 = 4

VECS = [("cond", 16), ("ada_b0", 48), ("ada_b1", 48), ("norm_g0", 16), ("norm_g1", 16),
        ("final_g", 8), ("q_g", 3), ("kv_g", 2), ("b_gf", 4), ("b_gb", 4), ("o_g", 2),
        ("mix_g0", 8), ("mix_g1", 8), ("ffn_g0", 8), ("ffn_g1", 8), ("final_g2", 8),
        ("lam_re", 8), ("lam_im", 8), ("log_dt", 8), ("s5_d", 2), ("b_glu", 2), ("v_g", 6),
        ("od_w", 24), ("od_b", 8), ("ffn_w0", 132), ("ffn_w1", 132), ("ffn_b0", 44), ("ffn_b1", 44)]
VAT, _at = {}, 0
for _n, _w in VECS:
    VAT[_n] = (_at, _w)
    _at += _w
NV = _at

NORMS = [("n0", 8, D, N), ("cq", 3, QR, N), ("ckv", 2, KVR, N), ("n1", 8, D, N)]
NORMS += [(f"o{h}", 2, GV, T) for h in range(GH)]
NORMS += [(n, 8, D, T) for n in ("f1", "mix0", "ffn0", "mix1", "ffn1", "f2")]
NI = {n[0]: i for i, n in enumerate(NORMS)}
NK = [sum(n[1] for n in NORMS[:i]) for i in range(len(NORMS) + 1)]
NA = [sum(n[1] - 1 for n in NORMS[:i]) for i in range(len(NORMS) + 1)]

SPLITS = [("n0", 8), ("cq", 3), ("ckv", 2), ("attn", 8), ("n1", 8)]
SPLITS += [(f"o{h}", 2) for h in range(GH)]
SPLITS += [("mix0", 8), ("gm", 6), ("s5", 2)]
for _l in range(2):
    SPLITS += ([("mix1", 8), ("od", 8)] if _l else [])
    SPLITS += [(f"ffn{_l}", 8), (f"act{_l}0", FH), (f"act{_l}1", FH)]
SAT, _at = {}, 0
for _n, _w in SPLITS:
    SAT[_n] = _at
    _at += _w

RESID = ["l0", "l1", "f1", "ev", "f00", "f01", "od", "f10", "f11"]
RAT = {n: 8 * i for i, n in enumerate(RESID)}

UNITS = [(h, q) for h in range(H) for q in range(TN)]
NU = len(UNITS)


def unit_keys(q):
    return list(range(TN)) if q < TX else list(range(TX, TN))


LOG_EXP = "natural_log_exp_and_others"
GV_AT, GG_AT = [0, 1, 2], [3, 4]
BACK = 5
SX_AT = [[0, 1, 2], [3, 4, 5], [6, 7]]
EV_K = [2, 3, 4, 5, 6, 7, 0, 1]


def here(places, l):
    return [i for i, at in enumerate(places) if at == l]


class Plan:

    def __init__(self):
        self.index, self.free, self.first, self.count = {}, [], [], []
        self.split, self.units, self.ada = [], [], 0
        self.last = {}
        n = 0

        def tile(key, free, weights=(), again=None):
            self.index[key] = len(self.free)
            self.free.append(free)
            start = len(self.split)
            if again is not None:
                start, weights_n = self.first[self.index[again]], self.count[self.index[again]]
            else:
                weights_n = len(weights)
                for w in weights:
                    if len(self.split) % UT == 0:
                        self.units.append(("split", len(self.split) // UT))
                    self.split.append(w)
            self.first.append(start)
            self.count.append(weights_n)
            for i in range(start, start + weights_n):
                self.last[("split", i // UT)] = len(self.free) - 1

        def ada(layer, j):
            for half in range(2):
                self.units.append(("raw", self.ada))
                self.last[("raw", self.ada)] = len(self.free)
                self.ada += 1
            tile(("ada", layer, j), [("arow", 12 * layer + j + 1)])

        def ada_t(layer, j):
            tile(("adaT", layer, j), [("mod", 12 * layer + j + 1)])

        def ktiles(name, m, k=KD):
            return [(name, i, m) for i in range(k)]

        def norm(name):
            tile(("ss", name), [("n_rs", 2 * NI[name] + 1)])

        for j in range(8):
            ada(0, j)
            if j:
                ada_t(0, j - 1)
        ada_t(0, 7)
        norm("n0")
        for m in range(5):
            tile(("c", m), [("craw", m + 1)], ktiles("win0", m))
        tile("kr", [("kr", 4)], ktiles("win0", 5))
        for m in range(8):
            tile(("gate0", m), [("gate0", m + 1)], ktiles("win0", 6 + m))
            if m == 1:
                norm("cq")
            if m == 3:
                norm("ckv")
        vt = [("uv", k, m) for k in range(2) for m in range(8)]
        for t in range(TN):
            tile(("v", t), [("v", t + 1)], vt, None if t == 0 else ("v", 0))

        def qk(h):
            tile(("Q", h), [("q_nope", h + 1), ("q_rope", 4 * h + 4)], [("uq", k, h) for k in range(3)])
            tile(("K", h), [("k_nope", h + 1)], [("uk", k, h) for k in range(2)])

        def score(u):
            tile(("S", u), [("p", u + 1)])

        more = [(0, j) for j in range(8, 12)] + [(1, j) for j in range(12)]
        qk(0)
        score(0)
        score(1)
        for u in range(NU):
            if u % TN == 1 and u // TN + 1 < H:
                qk(u // TN + 1)
            if u % TN == 3:
                ada(*more[u // TN])
            if u % TN == 5:
                ada_t(*more[u // TN])
            if u + 2 < NU:
                score(u + 2)
            tile(("PT", u), [("pt", u + 1)])
            if u:
                tile(("O", u - 1), [("o", u)])
        tile(("O", NU - 1), [("o", NU)])
        for m in range(8):
            tile(("OT", m), [("hf", SAT["attn"] + m + 1)])
        for m in range(8):
            tile(("l0", m), [("residc", m + 1)], ktiles("wout0", m))
        norm("n1")
        tile("r", [("gr", 1)], ktiles("gr", 0))
        def decay(h, d):
            tile((("gf", "gb")[d], h), [("g_min", 2 * h + d + 1), ("g_log", 6 * h + 3 * d + 1)])

        tile(("gq", 0), [("gq", 1)], ktiles("gin", 0))
        decay(0, 0)
        decay(0, 1)
        for h in range(GH):
            tile(("gk", h), [("gk", h + 1)], ktiles("gin", 4 + h))
            w = [("gin", k, 8 + 2 * h + m) for k in range(KD) for m in range(2)]
            for l in range(8):
                for t in here(GV_AT, l):
                    tile(("gv", h, t), [("gv", 3 * h + t + 1)], w, None if t == 0 else ("gv", h, 0))
                for m in here(GG_AT, l):
                    tile(("gg", h, m), [("gg", 2 * h + m + 1)], ktiles("gin", 16 + 2 * h + m))
                tile(("lev", h, l), [("lev", 8 * h + l + 1)])
            if h + 1 < GH:
                tile(("gq", h + 1), [("gq", h + 2)], ktiles("gin", h + 1))
            for d in range(2):
                tile(("kT", h, d), [("kT", 2 * h + d + 1)])
            for d in range(2):
                tile(("st", h, d), [("st", 8 * h + 4 * d + 4)])
            for m in range(2):
                tile(("go", h, m), [("go", 2 * h + m + 1)])
            if h + 1 < GH:
                decay(h + 1, 0)
            norm(f"o{h}")
            if h + 1 < GH:
                decay(h + 1, 1)
        for m in range(8):
            tile(("l1", m), [("resid", RAT["l1"] + m + 1)], ktiles("wout1", m))
        norm("f1")
        norm("mix0")
        for m in range(2):
            tile(("su", m), [("su", m + 1)], ktiles("ein", m))
        for w in range(3):
            for j in SX_AT[w]:
                tile(("sx", j), [("sx", j + 1)])
            wt = [("ein", k, 8 + 2 * w + m) for k in range(KD) for m in range(2)]
            tile(("mv", w), [("mv", w + 1)], wt)
        for m in range(GM):
            tile(("mu", m), [("mu", m + 1)], ktiles("ein", 2 + m))
        for m in range(GM):
            tile(("mg", m), [("mg", m + 1)])
        for c in range(2):
            tile(("sy", c), [("sy", c + 1)])
        for c in range(2):
            tile(("glu", c), [("glu", c + 1)])
        for m in range(8):
            tile(("ev", m), [("resid", RAT["ev"] + m + 1)],
                 [("eout", k, m) for k in EV_K])

        def ffn(l):
            norm(f"ffn{l}")
            for f in range(2):
                for j in range(FH):
                    tile(("up", l, f, j), [("conv", 4 * ((2 * l + f) * FH + j + 1))],
                         ktiles(f"up{l}", f * FH + j) + ktiles(f"up{l}", 2 * FH + f * FH + j))
                for m in range(8):
                    tile(("dn", l, f, m), [("resid", RAT[f"f{l}{f}"] + m + 1)],
                         [(f"dn{l}", f * FH + k, m) for k in range(FH)])

        ffn(0)
        norm("mix1")
        for m in range(8):
            tile(("ch", m), [("ch", m + 1)], ktiles("oin", 8 + m) + ktiles("oin", 16 + m))
            tile(("bg", m), [("hf", SAT["od"] + m + 1)], ktiles("oin", m))
        for m in range(8):
            tile(("od", m), [("resid", RAT["od"] + m + 1)], ktiles("oout", m))
        ffn(1)
        norm("f2")
        self.nsplit = -(-len(self.split) // UT)
        self.unit_at = {u: i for i, u in enumerate(self.units)}
        self.load_after, most = [], -1
        for c in range(len(self.units)):
            if c >= RAW and self.units[c - RAW][0] == "raw":
                most = max(most, self.last[self.units[c - RAW]])
            self.load_after.append(most)
        self.first_use = {}
        for n, (s, c) in enumerate(zip(self.first, self.count, strict=True)):
            for i in range(s, s + c):
                self.first_use.setdefault(i // UT, n)


PLAN = Plan()



class Serial:

    def __init__(self, engine, sem, own):
        self.engine, self.sem, self.own, self.counts = engine, sem, own, {}

    def __call__(self, instruction, name=None):
        name = name or self.own
        self.counts[name] = self.counts.get(name, 0) + 1
        instruction.then_inc(self.sem(name), 1)
        self.engine.wait_ge(self.sem(name), self.counts[name])


def hf_of(j):
    return SAT[f"act{j // (2 * FH)}{j // FH % 2}"] + j % FH + 1


def build(nc, a):
    fp32, fp22 = mybir.dt.float32, mybir.dt.float32r
    ALU, ACT, AX = mybir.AluOpType, mybir.ActivationFunctionType, mybir.AxisListType
    plan = PLAN
    ctx = ExitStack()
    sems = {}

    def sem(name):
        if name not in sems:
            sems[name] = ctx.enter_context(nc.semaphore("s_" + name))
        return sems[name]

    def sb(name, shape, dt=fp32):
        return ctx.enter_context(nc.sbuf_tensor(name, [P] + shape, dt))

    def place(at, name, shape, dt=fp32):
        scope = ExitStack()
        if at:
            scope.enter_context(nc.sbuf_tensor(f"before_{name}", [P, at], fp32))
        t = scope.enter_context(nc.sbuf_tensor(name, [P] + shape, dt))
        scope.close()
        return t

    with ctx:
        PS = [ctx.enter_context(nc.psum_tensor(f"ps{i}", [P, 1024], fp32)) for i in range(BANKS2)]
        raw = sb("raw", [RAW, UT * P])
        whi, wlo = sb("whi", [CONV, UT * P], fp22), sb("wlo", [CONV, UT * P], fp22)
        X = sb("X", [KD, T])
        vec = sb("vec", [NV])
        ident, ones = sb("ident", [P]), sb("ones", [2 * P])
        hf = sb("hf", [2, N])
        sq = sb("sq", [3, N])
        acc, rstd = sb("acc", [N]), sb("rstd", [N])
        small2 = sb("small2", [2])
        eps1 = sb("eps1", [2])
        mod = sb("mod", [2, 48])
        sc1 = sb("sc1", [2, 16])
        cnd = sb("cnd", [16])
        CX = place(0, "CX", [KD, TC])
        rope = place(2048, "rope", [T])
        gate0 = place(2560, "gate0", [KD, N])
        Hhi, Hlo = place(8704, "Hhi", [KD, N], fp22), place(14848, "Hlo", [KD, N], fp22)
        V, O = place(8704, "V", [TN, D]), place(14848, "O", [TN, D])
        Chi, Clo = place(20992, "Chi", [5, N], fp22), place(24832, "Clo", [5, N], fp22)
        craw = place(28672, "craw", [5, N])
        Q, Pr, PT, K = (place(28672 + 1536 * i, n, [2, N]) for i, n in enumerate(["Q", "Pr", "PT", "K"]))
        small = place(34816, "small", [3, 8])
        Ahi, Alo = place(20992, "Ahi", [KD, N], fp22), place(27136, "Alo", [KD, N], fp22)
        gR, masks = place(33280, "gR", [N]), place(34048, "masks", [8, P])
        ghi, glo = place(2048, "ghi", [KD, T], fp22), place(6144, "glo", [KD, T], fp22)
        wg = place(10240, "wg", [2, 512])
        gv, S = place(11264, "gv", [TN, GV]), place(12800, "S", [2, 4, GV])
        ex = place(14848, "ex", [2, 2, T])
        gk, bF, nB = (place(16896 + N * i, n, [N]) for i, n in enumerate(["gk", "bF", "nB"]))
        kT = place(19200, "kT", [N])
        gG = place(19968, "gG", [2, T])
        gq, At, Am = (place(T * i, n, [T]) for i, n in enumerate(["gq", "At", "Am"]))
        edge = place(3 * T, "edge", [20])
        Fhi, Flo = place(0, "Fhi", [FH, T], fp22), place(5632, "Flo", [FH, T], fp22)
        cv = place(11264, "cv", [3, 2, T])
        tmp = place(33280, "tmp", [2, 2 * T])
        lB, lC = place(0, "lB", [2, 2, P]), place(512, "lC", [2, SG, 32])
        glw = place(1024, "glw", [2, SW])
        gmw, bs = place(1536, "gmw", [GM, P]), place(2304, "bs", [GM, P])
        U = place(3072, "U", [2, T])
        wS = place(4096, "wS", [TX, 2, SG, P])
        mst = place(12288, "mst", [TX])
        mV, mU = place(12544, "mV", [TX, GM * P]), place(15616, "mU", [GM, T])
        tab = place(18688, "tab", [2, SG, P])
        sp = place(20736, "sp", [32, SG])
        spare = place(20992, "spare", [KD, N])
        step = tmp[:, 0, :]
        level_ex = [ex[:, 0, :, :], ex[:, 1, :, :],
                    sq[:, :, :].rearrange("p a t -> p (a t)")[:, 0:2 * T].rearrange("p (i t) -> p i t", i=2)]
        decayed_kT = [kT[:, :], sq[:, 0, :]]
        wtmp = sq[:, :, :].rearrange("p a t -> p (a t)")[:, 0:2 * T]

        def v_(name, i=0, n=1):
            return vec[:, VAT[name][0] + i:VAT[name][0] + i + n]

        block = ctx.enter_context(nc.Block())

        split_at = []

        @block.sync
        def _(sy):
            ns = {}
            for c, (kind, i) in enumerate(plan.units):
                if c >= RAW:
                    was, j = plan.units[c - RAW]
                    if was == "split":
                        sy.wait_ge(sem("wlo"), j + 1)
                    else:
                        sy.wait_ge(sem("psum"), plan.last[(was, j)] + 1)
                sy.dma_start(raw[:, c % RAW, :], a["units"][c]).then_inc(sem(f"ld{c % RAW}"), 16)
            for k in range(KD):
                sy.wait_ge(sem("out"), k + 1)
                sy.dma_start(a["out"][:, k, :], X[:, k, :]).then_inc(sem("stored"), 16)
            sy.wait_ge(sem("stored"), 16 * KD)

        @block.tensor
        def _(pe):
            at = [0]

            def tile(key):
                n = plan.index[key]
                assert n == at[0], (key, n, at[0])
                at[0] += 1
                if n >= BANKS2:
                    for name, value in plan.free[n - BANKS2]:
                        pe.wait_ge(sem(name), value)
                return PS[n % BANKS2]

            def done(last):
                last.then_inc(sem("psum"), 1)

            seen = [-1]

            def weights(key, i, n=P):
                w = plan.first[plan.index[key]] + i
                s, j = w // UT, w % UT
                if s > seen[0]:
                    pe.wait_ge(sem("wlo"), s + 1)
                    seen[0] = s
                return (x[:, s % CONV, j * P:j * P + n] for x in (whi, wlo))

            def product(out, stat, mov, first, last):
                (sh, sl), (mh, ml) = stat, mov
                nc.tensor.matmul(out, sh, mh, start=first, stop=False)
                nc.tensor.matmul(out, sh, ml, start=False, stop=False)
                return nc.tensor.matmul(out, sl, mh, start=False, stop=last)

            def linear(key, hi, lo, k_at, ready, cols, offset=0, ks=None, col0=0):
                ps = PS[plan.index[key] % BANKS2]
                ks = ks or list(range(plan.count[plan.index[key]]))
                for i, k in enumerate(ks):
                    if ready is not None:
                        pe.wait_ge(sem("lo"), ready + i)
                    w = tuple(weights(key, offset + i))
                    for c0, c1 in cols:
                        last = product(ps[:, col0 + c0:col0 + c1], w, (hi[:, k_at + k, c0:c1], lo[:, k_at + k, c0:c1]),
                                       i == 0, i == len(ks) - 1)
                return last

            def norm(name):
                _, k, _, n = NORMS[NI[name]]
                ps = tile(("ss", name))
                pe.wait_ge(sem("n_acc"), NA[NI[name] + 1])
                for c0 in range(0, n, T):
                    last = nc.tensor.matmul(ps[:, c0:min(n, c0 + T)], ones[:, 0:P], acc[:, c0:min(n, c0 + T)],
                                            start=True, stop=True)
                done(last)

            def ada(layer, j):
                ps = tile(("ada", layer, j))
                for m in range(2):
                    n = 24 * layer + 2 * j + m
                    c = plan.unit_at[("raw", n)]
                    pe.wait_ge(sem(f"ld{c % RAW}"), 16 * (c // RAW + 1))
                    for k in range(KD):
                        last = nc.tensor.matmul(ps[0:2, m * P:(m + 1) * P], cnd[:, 2 * k:2 * k + 2],
                                                raw[:, c % RAW, k * P:(k + 1) * P], start=k == 0, stop=k == KD - 1)
                done(last)

            def ada_t(layer, j):
                ps = tile(("adaT", layer, j))
                pe.wait_ge(sem("arow"), 12 * layer + j + 1)
                for m in range(2):
                    last = nc.tensor.transpose(ps[:, 2 * m:2 * m + 2], hf[0:2, j % 2, m * P:(m + 1) * P], ident[0:2, 0:2])
                done(last)

            BOTH, XO = [(0, T), (T, N)], [(0, T)]
            pe.wait_ge(sem("cnd"), 1)
            for j in range(8):
                ada(0, j)
                if j == 0:
                    pe.wait_ge(sem("consts"), 16 * 4)
                else:
                    ada_t(0, j - 1)
            ada_t(0, 7)
            pe.wait_ge(sem("ones"), 2)
            norm("n0")
            for m in range(5):
                tile(("c", m))
                done(linear(("c", m), Hhi, Hlo, 0, SAT["n0"] + 1, BOTH))
            tile("kr")
            done(linear("kr", Hhi, Hlo, 0, None, BOTH))
            for m in range(8):
                tile(("gate0", m))
                done(linear(("gate0", m), Hhi, Hlo, 0, None, BOTH))
                if m == 1:
                    norm("cq")
                if m == 3:
                    norm("ckv")
            pe.wait_ge(sem("lo"), SAT["ckv"] + 2)
            for t in range(TN):
                ps = tile(("v", t))
                for half in range(2):
                    for k in range(2):
                        w = tuple(weights(("v", t), 8 * k + 4 * half, 512))
                        tok = tuple(x[:, 3 + k, t * P:(t + 1) * P] for x in (Chi, Clo))
                        last = product(ps[:, 512 * half:512 * half + 512], tok, w, k == 0, k == 1)
                done(last)

            def qk(h):
                tile(("Q", h))
                done(linear(("Q", h), Chi, Clo, 0, None, BOTH))
                tile(("K", h))
                done(linear(("K", h), Chi, Clo, 3, None, BOTH))

            def score(u):
                h, q = UNITS[u]
                ps = tile(("S", u))
                if q == 0:
                    pe.wait_ge(sem("q_nope"), h + 1)
                    pe.wait_ge(sem("q_rope"), 4 * h + 4)
                    pe.wait_ge(sem("k_nope"), h + 1)
                    pe.wait_ge(sem("kr"), 6)
                for c0, c1 in (BOTH if q < TX else [(T, N)]):
                    o0 = c0 if q < TX else 0
                    last = nc.tensor.matmul(ps[:, o0:o0 + c1 - c0], Q[0:96, h % 2, q * P:(q + 1) * P],
                                            K[0:96, h % 2, c0:c1], start=True, stop=True)
                done(last)

            def out(u):
                h, q = UNITS[u]
                ps = tile(("O", u))
                pe.wait_ge(sem("pt"), u + 1)
                keys = unit_keys(q)
                for i, t in enumerate(keys):
                    last = nc.tensor.matmul(ps[:, 0:HV], PT[:, u % 2, i * P:(i + 1) * P],
                                            V[:, t, h * HV:(h + 1) * HV], start=i == 0, stop=i == len(keys) - 1)
                done(last)

            pe.wait_ge(sem("v"), TN)
            more = [(0, j) for j in range(8, 12)] + [(1, j) for j in range(12)]
            qk(0)
            score(0)
            score(1)
            for u in range(NU):
                if u % TN == 1 and u // TN + 1 < H:
                    qk(u // TN + 1)
                if u % TN == 3:
                    ada(*more[u // TN])
                if u % TN == 5:
                    ada_t(*more[u // TN])
                if u + 2 < NU:
                    score(u + 2)
                ps = tile(("PT", u))
                pe.wait_ge(sem("p"), u + 1)
                for i in range(len(unit_keys(UNITS[u][1]))):
                    last = nc.tensor.transpose(ps[:, i * P:(i + 1) * P], Pr[:, u % 2, i * P:(i + 1) * P], ident[:, :])
                done(last)
                if u:
                    out(u - 1)
            out(NU - 1)
            for m in range(8):
                ps = tile(("OT", m))
                pe.wait_ge(sem("o"), NU)
                for t in range(TN):
                    last = nc.tensor.transpose(ps[:, t * P:(t + 1) * P], O[:, t, m * P:(m + 1) * P], ident[:, :])
                done(last)
            for m in range(8):
                tile(("l0", m))
                done(linear(("l0", m), Ahi, Alo, 0, SAT["attn"] + 1, BOTH))
            norm("n1")
            tile("r")
            done(linear("r", Ahi, Alo, 0, SAT["n1"] + 1, BOTH))
            def queries(h):
                tile(("gq", h))
                done(linear(("gq", h), Ahi, Alo, 0, None, XO))

            def decay(h, d):
                ps = tile((("gf", "gb")[d], h))
                pe.wait_ge(sem("gr"), 1)
                pe.wait_ge(sem("glc"), 32)
                for c0, c1 in BOTH:
                    last = nc.tensor.matmul(ps[:, c0:c1], wg[0:32, d, h * P:(h + 1) * P], gR[0:32, c0:c1],
                                            start=True, stop=True)
                done(last)

            queries(0)
            decay(0, 0)
            decay(0, 1)
            for h in range(GH):
                tile(("gk", h))
                done(linear(("gk", h), Ahi, Alo, 0, None, BOTH))
                for l in range(8):
                    for t in here(GV_AT, l):
                        ps = tile(("gv", h, t))
                        for i in range(2):
                            for k in range(KD):
                                w = tuple(weights(("gv", h, t), 2 * k, GV))
                                tok = tuple(x[:, k, (2 * t + i) * P:(2 * t + i + 1) * P] for x in (Ahi, Alo))
                                last = product(ps[:, i * GV:(i + 1) * GV], tok, w, k == 0, k == KD - 1)
                        done(last)
                    for m in here(GG_AT, l):
                        tile(("gg", h, m))
                        done(linear(("gg", h, m), Ahi, Alo, 0, None, XO))
                    ps = tile(("lev", h, l))
                    if l == 0:
                        pe.wait_ge(sem("gq"), h + 1)
                        pe.wait_ge(sem("gk"), h + 1)
                        kk, qq = gk, gq
                    else:
                        pe.wait_ge(sem("lq"), 14 * h + 2 * l)
                        kk, qq = level_ex[l % 3][:, 1, :], level_ex[l % 3][:, 0, :]
                    for c in range(TX):
                        s = slice(c * P, (c + 1) * P)
                        last = nc.tensor.matmul(ps[:, s], kk[:, s], qq[:, s], start=True, stop=True)
                    done(last)
                if h + 1 < GH:
                    queries(h + 1)
                for d in range(2):
                    ps = tile(("kT", h, d))
                    pe.wait_ge(sem("kd"), 2 * h + d + 1)
                    kdec = ex[:, d, :, :].rearrange("p a t -> p (a t)")
                    for t in range(TN):
                        last = nc.tensor.transpose(ps[:, t * P:(t + 1) * P], kdec[:, t * P:(t + 1) * P], ident[:, :])
                    done(last)
                for d in range(2):
                    ps = tile(("st", h, d))
                    pe.wait_ge(sem("kT"), 2 * h + d + 1)
                    pe.wait_ge(sem("gv"), 3 * h + 3)
                    for i, ts in enumerate([[4, 5], [0], [1], [2]] if d == 0 else [[4, 5], [3], [2], [1]]):
                        for t in ts:
                            last = nc.tensor.matmul(ps[:, i * GV:(i + 1) * GV], decayed_kT[d][:, t * P:(t + 1) * P], gv[:, t, :],
                                                    start=t == ts[0], stop=t == ts[-1])
                    done(last)
                qd = ex[:, 0, :, :]
                for m in range(2):
                    ps = tile(("go", h, m))
                    pe.wait_ge(sem("qd"), 2 * h + 2)
                    pe.wait_ge(sem("st"), 8 * h + 8)
                    pe.wait_ge(sem("ladd"), 7 * h + 7)
                    for c in range(TX):
                        s, f = slice(c * P, (c + 1) * P), slice(m * P, (m + 1) * P)
                        nc.tensor.matmul(ps[:, s], gv[:, c, f], At[:, s], start=True, stop=False)
                        nc.tensor.matmul(ps[:, s], S[:, 0, c, f], qd[:, 0, s], start=False, stop=False)
                        last = nc.tensor.matmul(ps[:, s], S[:, 1, c, f], qd[:, 1, s], start=False, stop=True)
                    done(last)
                if h + 1 < GH:
                    decay(h + 1, 0)
                norm(f"o{h}")
                if h + 1 < GH:
                    decay(h + 1, 1)
            for m in range(8):
                tile(("l1", m))
                done(linear(("l1", m), ghi, glo, 0, SAT["o0"] + 1, XO))
            norm("f1")
            norm("mix0")

            def s5_in(j):
                ps = tile(("sx", j))
                pe.wait_ge(sem("su"), j // 4 + 1)
                pe.wait_ge(sem("s5c"), 16 * 3)
                r = slice(32 * (j % 4), 32 * (j % 4) + 32)
                for i in range(2):
                    last = nc.tensor.matmul(ps[:, i * T:(i + 1) * T], lB[r, j // 4, i, :], U[r, j // 4, :],
                                            start=True, stop=True)
                done(last)

            for m in range(2):
                tile(("su", m))
                done(linear(("su", m), Ahi, Alo, 0, SAT["mix0"] + 1, XO))
            for w in range(3):
                for j in SX_AT[w]:
                    s5_in(j)
                ps = tile(("mv", w))
                for t in range(TX):
                    for k in range(KD):
                        wt = tuple(weights(("mv", w), 2 * k, 2 * P))
                        tok = tuple(x[:, k, t * P:(t + 1) * P] for x in (Ahi, Alo))
                        last = product(ps[:, t * 256:(t + 1) * 256], tok, wt, k == 0, k == KD - 1)
                done(last)
            for m in range(GM):
                tile(("mu", m))
                done(linear(("mu", m), Ahi, Alo, 0, None, XO))
            for m in range(GM):
                ps = tile(("mg", m))
                pe.wait_ge(sem("mvn"), TX)
                pe.wait_ge(sem("gmw"), 1)
                for t in range(TX):
                    last = nc.tensor.matmul(ps[:, t * P:(t + 1) * P], mV[:, t, m * P:(m + 1) * P], gmw[:, m, :],
                                            start=True, stop=True)
                done(last)
            for c in range(2):
                ps = tile(("sy", c))
                pe.wait_ge(sem("lZ"), 2)
                for j in range(4 * c, 4 * c + 4):
                    pe.wait_ge(sem("sh" if j < BACK else "shp"), j + 1 if j < BACK else j + 1 - BACK)
                    r = slice(32 * (j % 4), 32 * (j % 4) + 32)
                    for i in range(2):
                        last = nc.tensor.matmul(ps[r, 0:T], lC[:, i, j, :], wS[:, :, i, j, :], start=i == 0, stop=i == 1)
                done(last)
            for c in range(2):
                ps = tile(("glu", c))
                pe.wait_ge(sem("y2"), 2)
                for k in range(2):
                    last = nc.tensor.matmul(ps[:, 0:T], glw[:, k, c * P:(c + 1) * P], U[:, k, :], start=k == 0, stop=k == 1)
                done(last)
            for m in range(8):
                tile(("ev", m))
                done(linear(("ev", m), Ahi, Alo, 0, SAT["gm"] + 1, XO, ks=EV_K))

            def ffn(l):
                norm(f"ffn{l}")
                for f in range(2):
                    for j in range(FH):
                        tile(("up", l, f, j))
                        for part in range(2):
                            last = linear(("up", l, f, j), Ahi, Alo, 0, SAT[f"ffn{l}"] + 1, XO, offset=KD * part,
                                          ks=list(range(KD)), col0=T * part)
                        done(last)
                    for m in range(8):
                        tile(("dn", l, f, m))
                        done(linear(("dn", l, f, m), Fhi, Flo, 0, SAT[f"act{l}{f}"] + 1, XO))

            ffn(0)
            norm("mix1")
            for m in range(8):
                tile(("ch", m))
                for part in range(2):
                    last = linear(("ch", m), Ahi, Alo, 0, SAT["mix1"] + 1, XO, offset=KD * part,
                                  ks=list(range(KD)), col0=T * part)
                done(last)
                tile(("bg", m))
                done(linear(("bg", m), Ahi, Alo, 0, None, XO))
            for m in range(8):
                tile(("od", m))
                done(linear(("od", m), Fhi, Flo, 0, SAT["od"] + 1, XO))
            ffn(1)
            norm("f2")
            assert at[0] == len(plan.free)

        @block.scalar
        def _(ac):
            for name in ("vec", "ident"):
                t = {"vec": vec, "ident": ident}[name]
                ac.dma_start(t[:, :], a[name]).then_inc(sem("consts"), 16)
            ac.dma_start(rope[:, :], a["rope"]).then_inc(sem("consts"), 16)
            ac.dma_start(eps1[:, :], a["eps1"]).then_inc(sem("consts"), 16)
            ac.dma_start(X[:, :, :], a["xT"]).then_inc(sem("xl"), 16)
            ac.dma_start(CX[:, :, :], a["ctxT"]).then_inc(sem("cl"), 16)
            nc.scalar.preload_act_table_set(LOG_EXP)
            do = Serial(ac, sem, "act")
            converted = [0]

            def convert(n):
                while converted[0] < plan.nsplit:
                    s = converted[0]
                    if s >= CONV and plan.last[("split", s - CONV)] > n:
                        break
                    c = plan.unit_at[("split", s)]
                    if plan.load_after[c] > n:
                        break
                    if plan.first_use[s] > n + AHEAD:
                        break
                    ac.wait_ge(sem(f"ld{c % RAW}"), 16 * (c // RAW + 1))
                    if s >= CONV:
                        ac.wait_ge(sem("psum"), plan.last[("split", s - CONV)] + 1)
                    nc.scalar.activation(whi[:, s % CONV, :], raw[:, c % RAW, :], ACT.Copy).then_inc(sem("whi"), 1)
                    converted[0] += 1
                    split_at.append(n)

            def psum(key):
                n = plan.index[key]
                convert(n - 1)
                ac.wait_ge(sem("psum"), n + 1)
                if key[0] in EAGER:
                    convert(n)
                return PS[n % BANKS2]

            def act(out, in_, f, bias=None, scale=1.0, sem_name=None, accum=None):
                kw = {} if accum is None else {"accum_out": accum}
                if bias is not None:
                    kw["bias"] = bias
                do(nc.scalar.activation(out, in_, f, scale=scale, **kw), sem_name)

            def squares(name, tiles, waits):
                i = NI[name]
                for k in range(NORMS[i][1]):
                    g = NK[i] + k
                    if g >= 3:
                        g3 = g - 3
                        j = max(x for x in range(len(NORMS)) if NK[x] <= g3)
                        ac.wait_ge(sem("n_acc"), NA[j] + max(1, g3 - NK[j]))
                    for name_, value in waits(k):
                        ac.wait_ge(sem(name_), value)
                    for src, c0, c1 in tiles(k):
                        act(sq[:, g % 3, c0:c1], src, ACT.Square, sem_name="n_sq")

            def root(name):
                i = NI[name]
                _, _, width, n = NORMS[i]
                nc.scalar.preload_act_table_set(LOG_EXP)
                ps = psum(("ss", name))
                if i:
                    ac.wait_ge(sem("n_use"), i)
                act(rstd[:, 0:n], ps[:, 0:n], ACT.Ln, eps1[:, 0:1], 1.0 / width, "n_rs")
                act(rstd[:, 0:n], rstd[:, 0:n], ACT.Exp, None, -0.5, "n_rs")

            split = [0]

            def high(dst):
                ac.wait_ge(sem("hf"), split[0] + 1)
                act(dst, hf[:, split[0] % 2, 0:dst.shape[-1]], ACT.Copy, sem_name="hi")
                split[0] += 1

            ac.wait_ge(sem("consts"), 64)
            act(cnd[:, :], v_("cond", 0, 16), ACT.Silu, sem_name="cnd")
            nc.scalar.preload_act_table_set(LOG_EXP)
            ac.wait_ge(sem("xl"), 16)
            ac.wait_ge(sem("cl"), 16)
            both = lambda k: [(X[:, k, :], 0, T), (CX[:, k, :], T, N)]
            only = lambda k: [(X[:, k, :], 0, T)]
            squares("n0", both, lambda k: [])
            root("n0")
            for k in range(KD):
                high(Hhi[:, k, :])
            for m in range(5):
                ps = psum(("c", m))
                act(craw[:, m, :], ps[:, 0:N], ACT.Copy, sem_name="craw")
            squares("cq", lambda k: [(craw[:, k, :], 0, N)], lambda k: [])
            squares("ckv", lambda k: [(craw[:, 3 + k, :], 0, N)], lambda k: [])
            psum("kr")
            for m in range(8):
                ps = psum(("gate0", m))
                act(gate0[:, m, :], ps[:, 0:N], ACT.Silu, sem_name="gate0")
                if m in (1, 3):
                    nc.scalar.preload_act_table_set(LOG_EXP)
                if m == 1:
                    root("cq")
                    for k in range(3):
                        high(Chi[:, k, :])
                if m == 3:
                    root("ckv")
                    for k in range(2):
                        high(Chi[:, 3 + k, :])
            for t in range(TN):
                ps = psum(("v", t))
                act(V[:, t, :], ps[:, :], ACT.Copy, sem_name="v")
            nc.scalar.preload_act_table_set(LOG_EXP)
            sc = float(NOPE + ROPE) ** -0.5

            def qk(h):
                ps = psum(("Q", h))
                act(Q[0:64, h % 2, :], ps[0:64, 0:N], ACT.Copy, sem_name="q_nope")
                ps = psum(("K", h))
                act(K[0:64, h % 2, :], ps[0:64, 0:N], ACT.Copy, None, sc, "k_nope")

            def softmax(u):
                n = P * len(unit_keys(UNITS[u][1]))
                ps = psum(("S", u))
                if u >= 2:
                    ac.wait_ge(sem("psum"), plan.index[("PT", u - 2)] + 1)
                ac.wait_ge(sem("mx"), u + 1)
                act(Pr[:, u % 2, 0:n], ps[:, 0:n], ACT.Exp, small[:, 0, u % 8:u % 8 + 1], 1.0, "p",
                    small[:, 1, u % 8:u % 8 + 1])

            qk(0)
            softmax(0)
            softmax(1)
            for u in range(NU):
                if u % TN == 1 and u // TN + 1 < H:
                    qk(u // TN + 1)
                if u + 2 < NU:
                    softmax(u + 2)
            for m in range(8):
                psum(("OT", m))
                high(Ahi[:, m, :])
            for m in range(8):
                psum(("l0", m))
            squares("n1", both, lambda k: [("resid", k + 1), ("residc", k + 1)])
            ac.dma_start(wg[0:32, :, :], a["wg"]).then_inc(sem("glc"), 16)
            ac.dma_start(masks[:, :, :], a["masks"]).then_inc(sem("glc"), 16)
            root("n1")
            for k in range(KD):
                high(Ahi[:, k, :])
            ps = psum("r")
            act(gR[0:32, :], ps[0:32, 0:N], ACT.Copy, sem_name="gr")
            def queries(h):
                ps = psum(("gq", h))
                act(gq[:, :], ps[:, 0:T], ACT.Copy, None, float(GK) ** -0.5, "gq")

            def level(h, l):
                ac.wait_ge(sem("le"), 28 * h + 4 * l)
                act(level_ex[l % 3], level_ex[l % 3], ACT.Exp, None, 1.0 / GATE_NORM, "lx")

            def decay(h, d):
                ps = psum((("gf", "gb")[d], h))
                e = ex[:, d, :, :].rearrange("p a t -> p (a t)")[:, 0:N]
                act(e, ps[:, 0:N], ACT.Abs, v_(("b_gf", "b_gb")[d], h), 1.0, "g_log")
                act(e, e, ACT.Exp, None, -1.0, "g_log")
                act(e, e, ACT.Ln, eps1[:, 1:2], 1.0, "g_log")

            queries(0)
            decay(0, 0)
            decay(0, 1)
            for h in range(GH):
                ps = psum(("gk", h))
                act(gk[:, :], ps[:, 0:N], ACT.Copy, sem_name="gk")
                for l in range(8):
                    for t in here(GV_AT, l):
                        ps = psum(("gv", h, t))
                        act(gv[:, 2 * t:2 * t + 2, :], ps[:, 0:T].rearrange("p (i v) -> p i v", i=2), ACT.Copy, sem_name="gv")
                    for m in here(GG_AT, l):
                        ps = psum(("gg", h, m))
                        act(gG[:, m, :], ps[:, 0:T], ACT.Copy, sem_name="gg")
                    if l < 7:
                        level(h, l + 1)
                ac.wait_ge(sem("edge"), 4 * h + 4)
                act(edge[:, 10:20], edge[:, 0:10], ACT.Exp, sem_name="kx")
                for d, (b, sign) in enumerate([(bF, -1.0), (nB, 1.0)]):
                    psum(("lev", h, 6 + d))
                    e = ex[:, d, :, :].rearrange("p a t -> p (a t)")
                    for c in range(5):
                        s = slice(c * P, (c + 1) * P) if c < 4 else slice(T, N)
                        act(e[:, s], b[:, s], ACT.Exp, edge[:, 5 * d + c:5 * d + c + 1], sign / GATE_NORM, "kx")
                ps = psum(("kT", h, 0))
                act(kT[:, :], ps[:, 0:N], ACT.Copy, sem_name="kT")
                act(ex[:, 0, 0, :], bF[:, 0:T], ACT.Exp, None, 1.0 / GATE_NORM, "qx")
                act(ex[:, 0, 1, :], nB[:, 0:T], ACT.Exp, None, -1.0 / GATE_NORM, "qx")
                ps = psum(("kT", h, 1))
                act(decayed_kT[1], ps[:, 0:N], ACT.Copy, sem_name="kT")
                act(gG[:, :, :], gG[:, :, :], ACT.Silu, sem_name="gs")
                if h + 1 < GH:
                    ac.wait_ge(sem("qd"), 2 * h + 2)
                    queries(h + 1)
                for m in range(2):
                    ps = psum(("go", h, m))
                    act(ex[:, 1, m, :], ps[:, 0:T], ACT.Copy, sem_name="go")
                squares(f"o{h}", lambda k: [(ex[:, 1, k, :], 0, T)], lambda k: [])
                nc.scalar.preload_act_table_set(LOG_EXP)
                if h + 1 < GH:
                    decay(h + 1, 0)
                root(f"o{h}")
                for m in range(2):
                    high(ghi[:, 2 * h + m, :])
                if h + 1 < GH:
                    decay(h + 1, 1)
            for t, n in [(lB, "lB"), (lC, "lC"), (glw, "glw")]:
                ac.dma_start(t[tuple([slice(None)] * len(t.shape))], a[n]).then_inc(sem("s5c"), 16)
            ac.wait_ge(sem("sp_a"), 1)
            act(sp[:, 1, :], v_("log_dt", 0, 8), ACT.Exp, sem_name="sp_b")
            ac.wait_ge(sem("sp_a"), 2)
            act(sp[:, 3, :], sp[:, 2, :], ACT.Exp, sem_name="sp_b")
            ac.wait_ge(sem("sp_a"), 3)
            act(sp[:, 7, :], sp[:, 6, :], ACT.Sin, sem_name="sp_b")
            act(sp[:, 8, :], sp[:, 9, :], ACT.Sin, sem_name="sp_b")
            nc.scalar.preload_act_table_set(LOG_EXP)
            for m in range(8):
                psum(("l1", m))
            squares("f1", only, lambda k: [("resid", RAT["l1"] + k + 1)])
            for t, n in [(gmw, "gmw"), (bs, "bs")]:
                ac.dma_start(t[tuple([slice(None)] * len(t.shape))], a[n]).then_inc(sem("evc"), 16)
            root("f1")
            squares("mix0", only, lambda k: [("resid", RAT["f1"] + k + 1)])
            root("mix0")
            for k in range(KD):
                high(Ahi[:, k, 0:T])
            for m in range(2):
                ps = psum(("su", m))
                act(U[:, m, :], ps[:, 0:T], ACT.Copy, sem_name="su")
            for w in range(3):
                for j in SX_AT[w]:
                    psum(("sx", j))
                ps = psum(("mv", w))
                act(mV[:, :, w * 256:(w + 1) * 256], ps[:, :].rearrange("p (t v) -> p t v", t=TX),
                    ACT.Gelu_apprx_tanh, sem_name="mv")
            nc.scalar.preload_act_table_set(LOG_EXP)
            for t in range(TX):
                act(hf[:, 0, 0:GM * P], mV[:, t, :], ACT.Square, None, 1.0, "mv_ss", mst[:, t:t + 1])
            act(mst[:, :], mst[:, :], ACT.Ln, eps1[:, 0:1], 1.0 / (GM * P), "mv_ss")
            act(mst[:, :], mst[:, :], ACT.Exp, None, -0.5, "mv_rs")
            for m in range(GM):
                ps = psum(("mu", m))
                act(mU[:, m, :], ps[:, 0:T], ACT.Gelu_apprx_tanh, sem_name="mu")
            for m in range(GM):
                psum(("mg", m))
                high(Ahi[:, 2 + m, 0:T])
            for c in range(2):
                psum(("sy", c))
                ac.wait_ge(sem("sy"), c + 1)
                act(U[:, c, :], U[:, c, :], ACT.Gelu_apprx_tanh, sem_name="y2")
            for c in range(2):
                ps = psum(("glu", c))
                act(tmp[:, 1, c * T:(c + 1) * T], ps[:, 0:T], ACT.Sigmoid, v_("b_glu", c), 1.0, "glu")
            for c in range(2):
                high(Ahi[:, c, 0:T])
            for m in range(8):
                psum(("ev", m))

            def ffn(l, before):
                squares(f"ffn{l}", only, lambda k: [("resid", RAT[before] + k + 1)])
                root(f"ffn{l}")
                for k in range(KD):
                    high(Ahi[:, k, 0:T])
                for f in range(2):
                    for r in range(FH + 2):
                        if r < FH:
                            ps = psum(("up", l, f, r))
                            j = (2 * l + f) * FH + r
                            if j >= 3:
                                ac.wait_ge(sem("hf"), hf_of(j - 3))
                            for part in range(2):
                                c = (part * 2 + f) * FH + r
                                act(cv[:, j % 3, part, :], ps[:, part * T:(part + 1) * T], ACT.Identity,
                                    v_(f"ffn_b{l}", c), v_(f"ffn_w{l}", 88 + c), "ca")
                        if 1 <= r <= FH:
                            j = (2 * l + f) * FH + r - 1
                            ac.wait_ge(sem("conv"), 4 * j + 4)
                            act(tmp[:, j % 2, 0:T], cv[:, j % 3, 0, :], ACT.Silu, sem_name="se")
                        if r >= 2:
                            high(Fhi[:, r - 2, :])
                    for m in range(8):
                        psum(("dn", l, f, m))

            ffn(0, "ev")
            squares("mix1", only, lambda k: [("resid", RAT["f01"] + k + 1)])
            root("mix1")
            for k in range(KD):
                high(Ahi[:, k, 0:T])
            for r in range(10):
                if r < 8:
                    ps = psum(("ch", r))
                    if r >= 3:
                        ac.wait_ge(sem("hf"), SAT["od"] + r - 2)
                    act(cv[:, r % 3, 0, :], ps[:, 0:T], ACT.Copy, sem_name="oc")
                if 1 <= r <= 8:
                    m = r - 1
                    ac.wait_ge(sem("ch"), m + 1)
                    act(tmp[:, m % 2, 0:T], cv[:, m % 3, 1, :], ACT.Identity, v_("od_b", m), v_("od_w", 16 + m), "oa")
                if r >= 2:
                    high(Fhi[:, r - 2, :])
            for m in range(8):
                psum(("od", m))
            ffn(1, "od")
            squares("f2", only, lambda k: [("resid", RAT["f11"] + k + 1)])
            root("f2")

        @block.gpsimd
        def _(po):
            def add(h, l):
                po.wait_ge(sem("lev"), 8 * h + l + 1)
                nc.gpsimd.tensor_tensor(At[:, :], At[:, :], Am[:, :], ALU.add).then_inc(sem("ladd"), 1)
                po.wait_ge(sem("ladd"), 7 * h + l)

            def turn_back(j):
                po.wait_ge(sem("scan"), 1)
                cs, sn = (tab[:, i, j:j + 1, :].to_broadcast([P, TX, P]) for i in range(2))
                re, im = (wS[:, :, i, j, :] for i in range(2))
                rc, ic, rs, is_ = (spare[:, i:i + TX, c:c + P] for i in (0, TX) for c in (T, T + P))
                for out, x, y, op in [(rc, re, cs, ALU.mult), (rs, re, sn, ALU.mult), (ic, im, cs, ALU.mult),
                                      (is_, im, sn, ALU.mult), (re, rc, is_, ALU.subtract), (im, ic, rs, ALU.add)]:
                    last = nc.gpsimd.tensor_tensor(out, x, y, op)
                    if out is not im:
                        turned[0] += 1
                        last.then_inc(sem("turn"), 1)
                        po.wait_ge(sem("turn"), turned[0])
                last.then_inc(sem("shp"), 1)

            turned = [0]
            sums = [(plan.index[("lev", h, l)], h, l) for h in range(GH) for l in range(1, 8)]
            masked = back = False
            for s in range(plan.nsplit):
                if not back and split_at[s] > plan.index[("mg", 1)]:
                    back = True
                    for j in range(BACK, SG):
                        turn_back(j)
                while sums and sums[0][0] < split_at[s]:
                    add(*sums.pop(0)[1:])
                po.wait_ge(sem("whi"), s + 1)
                nc.gpsimd.tensor_tensor(wlo[:, s % CONV, :], raw[:, plan.unit_at[("split", s)] % RAW, :],
                                        whi[:, s % CONV, :].bitcast(fp32), ALU.subtract).then_inc(sem("wlo"), 1)
                if not masked and s * UT >= plan.first[plan.index[("mv", 0)]]:
                    masked = True
                    po.wait_ge(sem("evc"), 16 * 2)
                    nc.gpsimd.affine_select(out=gmw[:, :, :], in_=gmw[:, :, :], compare_op=ALU.is_ge, fill=0.0,
                                            base=0, pattern=[[0, GM], [1, P]], channel_multiplier=-1)\
                        .then_inc(sem("gmw"), 1)

        @block.vector
        def _(ve):
            do = Serial(ve, sem, "dve")
            TTi, TSi, STTi = nc.vector.tensor_tensor, nc.vector.tensor_scalar, nc.vector.scalar_tensor_tensor

            def tt(out, x, y, op, s=None):
                do(TTi(out, x, y, op), s)

            def ts(out, x, s1, s2, op0, op1=None, s=None):
                do(TSi(out, x, s1, s2, op0, op1) if op1 is not None else TSi(out, x, s1, None, op0), s)

            def stt(out, x, sc, y, op0, op1, s=None):
                do(STTi(out, x, sc, y, op0, op1), s)

            def psum(key):
                ve.wait_ge(sem("psum"), plan.index[key] + 1)
                return PS[plan.index[key] % BANKS2]

            ADD, SUB, MUL, MAX, MIN = ALU.add, ALU.subtract, ALU.mult, ALU.max, ALU.min
            nsq = [0]

            def sums(name):
                i = NI[name]
                _, k_, _, n = NORMS[i]
                per = 2 if name in ("n0", "n1") else 1
                if i:
                    ve.wait_ge(sem("psum"), plan.index[("ss", NORMS[i - 1][0])] + 1)
                for k in range(1, k_):
                    ve.wait_ge(sem("n_sq"), nsq[0] + per * (k + 1))
                    g = NK[i] + k
                    first = sq[:, (g - 1) % 3, 0:n] if k == 1 else acc[:, 0:n]
                    tt(acc[:, 0:n], first, sq[:, g % 3, 0:n], ADD, "n_acc")
                nsq[0] += per * k_

            made, waiting = [0], []

            def low():
                dst, i = waiting.pop(0)
                hi, lo = dst
                ve.wait_ge(sem("hi"), i + 1)
                tt(lo, hf[:, i % 2, 0:lo.shape[-1]], hi.bitcast(fp32), SUB, "lo")

            def to_split(n):
                if len(waiting) == 2:
                    low()
                return hf[:, made[0] % 2, 0:n]

            def queued(hi, lo):
                waiting.append(((hi, lo), made[0]))
                made[0] += 1

            def flush():
                while waiting:
                    low()

            def apply(name, src, gain, hi, lo, n, extra=None):
                i = NI[name]
                ve.wait_ge(sem("n_rs"), 2 * i + 2)
                for k in range(NORMS[i][1]):
                    b = to_split(n)
                    if extra is None:
                        stt(b, src(k), gain(k), rstd[:, 0:n], MUL, MUL, "hf")
                    else:
                        stt(b, src(k), gain(k), rstd[:, 0:n], MUL, MUL)
                        tt(b, b, extra(k), MUL, "hf")
                    queued(hi(k), lo(k))
                flush()
                ts(small2[:, 0:1], eps1[:, 0:1], 1.0, None, MUL, s="n_use")

            def modulated(name, layer, hi, lo):
                i = NI[name]
                ve.wait_ge(sem("n_rs"), 2 * i + 2)
                for k in range(KD):
                    b = to_split(N)
                    for c, (src, s) in enumerate([(X, slice(0, T)), (CX, slice(T, N))]):
                        tt(b[:, s], src[:, k, :], rstd[:, s], MUL)
                        ts(b[:, s], b[:, s], sc1[:, layer, 2 * k + c:2 * k + c + 1], mod[:, layer, 2 * k + c:2 * k + c + 1],
                           MUL, ADD, s="hf" if c else None)
                    queued(hi[:, k, :], lo[:, k, :])
                flush()
                ts(small2[:, 0:1], eps1[:, 0:1], 1.0, None, MUL, s="n_use")

            def ada(layer, j):
                ps = psum(("ada", layer, j))
                do(nc.vector.tensor_copy(hf[0:2, j % 2, 0:2 * P], ps[0:2, 0:2 * P]), "arow")

            def ada_t(layer, j):
                ps = psum(("adaT", layer, j))
                tt(mod[:, layer, 4 * j:4 * j + 4], ps[:, 0:4], v_(f"ada_b{layer}", 4 * j, 4), ADD, "mod")

            def scales(layer):
                stt(sc1[:, layer, :], mod[:, layer, 16:32], 1.0, v_(f"norm_g{layer}", 0, 16), ADD, MUL)

            do(nc.vector.memset(ones[:, :], 1.0), "ones")
            do(nc.vector.memset(small2[:, :], 0.0), "ones")
            ve.wait_ge(sem("consts"), 64)
            sums("n0")
            for j in range(8):
                ada(0, j)
                if j:
                    ada_t(0, j - 1)
            ada_t(0, 7)
            scales(0)
            modulated("n0", 0, Hhi, Hlo)
            ve.wait_ge(sem("craw"), 5)
            sums("cq")
            ps = psum("kr")
            r, r2 = slice(64, 96), slice(96, 128)
            sc = float(NOPE + ROPE) ** -0.5
            tt(K[r, 0, 0:T], ps[r, 0:T], rope[r, :], MUL, "kr")
            tt(PT[r, 1, 0:T], ps[r2, 0:T], rope[r2, :], MUL, "kr")
            tt(K[r, 0, 0:T], K[r, 0, 0:T], PT[r, 1, 0:T], ADD, "kr")
            do(nc.vector.tensor_copy(K[r, 0, T:N], ps[r, T:N]), "kr")
            ts(K[r, 0, :], K[r, 0, :], sc, None, MUL, s="kr")
            do(nc.vector.tensor_copy(K[r, 1, :], K[r, 0, :]), "kr")
            apply("cq", lambda k: craw[:, k, :], lambda k: v_("q_g", k), lambda k: Chi[:, k, :],
                  lambda k: Clo[:, k, :], N)
            sums("ckv")
            apply("ckv", lambda k: craw[:, 3 + k, :], lambda k: v_("kv_g", k), lambda k: Chi[:, 3 + k, :],
                  lambda k: Clo[:, 3 + k, :], N)

            def q_rope(h):
                ps = psum(("Q", h))
                ve.wait_ge(sem("q_nope"), h + 1)
                tt(Q[r, h % 2, 0:T], ps[r, 0:T], rope[r, :], MUL, "q_rope")
                tt(acc[r, 0:T], ps[r2, 0:T], rope[r2, :], MUL, "q_rope")
                tt(Q[r, h % 2, 0:T], Q[r, h % 2, 0:T], acc[r, 0:T], ADD, "q_rope")
                do(nc.vector.tensor_copy(Q[r, h % 2, T:N], ps[r, T:N]), "q_rope")

            def row_max(u):
                n = P * len(unit_keys(UNITS[u][1]))
                ps = psum(("S", u))
                do(nc.vector.tensor_reduce(small[:, 0, u % 8:u % 8 + 1], ps[:, 0:n], AX.X, MAX, negate=True), "mx")

            def out(u):
                h, q = UNITS[u]
                ve.wait_ge(sem("p"), u + 1)
                do(nc.vector.reciprocal(small[:, 2, u % 8:u % 8 + 1], small[:, 1, u % 8:u % 8 + 1]))
                ps = psum(("O", u))
                ts(O[:, q, h * HV:(h + 1) * HV], ps[:, 0:HV], small[:, 2, u % 8:u % 8 + 1], None, MUL, s="o")

            more = [(0, j) for j in range(8, 12)] + [(1, j) for j in range(12)]
            q_rope(0)
            row_max(0)
            row_max(1)
            for u in range(NU):
                if u % TN == 1 and u // TN + 1 < H:
                    q_rope(u // TN + 1)
                if u % TN == 3:
                    ada(*more[u // TN])
                if u % TN == 5:
                    ada_t(*more[u // TN])
                if u + 2 < NU:
                    row_max(u + 2)
                n = P * len(unit_keys(UNITS[u][1]))
                ps = psum(("PT", u))
                do(nc.vector.tensor_copy(PT[:, u % 2, 0:n], ps[:, 0:n]), "pt")
                if u:
                    out(u - 1)
            out(NU - 1)
            scales(1)
            for m in range(8):
                ps = psum(("OT", m))
                b = to_split(N)
                ve.wait_ge(sem("gate0"), m + 1)
                tt(b, ps[:, 0:N], gate0[:, m, :], MUL, "hf")
                queued(Ahi[:, m, :], Alo[:, m, :])
            flush()

            def resid(key, m, gate=None, n_sem="resid"):
                ps = psum(key)
                if gate is None:
                    tt(X[:, m, :], ps[:, 0:T], X[:, m, :], ADD, n_sem)
                else:
                    stt(X[:, m, :], ps[:, 0:T], gate, X[:, m, :], MUL, ADD, n_sem)

            for m in range(8):
                resid(("l0", m), m, mod[:, 0, 32 + 2 * m:33 + 2 * m])
                ps = psum(("l0", m))
                stt(CX[:, m, :], ps[:, T:N], mod[:, 0, 33 + 2 * m:34 + 2 * m], CX[:, m, :], MUL, ADD, "residc")
            sums("n1")
            modulated("n1", 1, Ahi, Alo)
            def decay(h, d):
                ps = psum((("gf", "gb")[d], h))
                b = (bF, nB)[d]
                ve.wait_ge(sem("g_log"), 6 * h + 3 * d + 1)
                ts(b[:, :], ps[:, 0:N], v_(("b_gf", "b_gb")[d], h), 0.0, ADD, MIN, s="g_min")
                ve.wait_ge(sem("g_log"), 6 * h + 3 * d + 3)
                tt(b[:, :], b[:, :], ex[:, d, :, :].rearrange("p a t -> p (a t)")[:, 0:N], SUB)
                pre = ex[:, 0, :, :].rearrange("p a t -> p (a t)")
                for c in range(5):
                    s = slice(c * P, (c + 1) * P) if c < 4 else slice(T, N)
                    w = s.stop - s.start
                    if d == 0:
                        do(nc.vector.tensor_tensor_scan(b[:, s], ones[:, 0:w], b[:, s], 0.0, MUL, ADD))
                    else:
                        do(nc.vector.tensor_tensor_scan(pre[:, s], ones[:, 0:w], b[:, s], 0.0, MUL, ADD))
                        stt(b[:, s], pre[:, s], pre[:, s.stop - 1:s.stop], b[:, s], SUB, SUB)

            decay(0, 0)
            decay(0, 1)
            for h in range(GH):
                ve.wait_ge(sem("kx"), 11 * h) if h else None
                k16 = 1.0 / GATE_NORM
                bx, nx = bF[:, 0:T].rearrange("p (c t) -> p c t", c=4), nB[:, 0:T].rearrange("p (c t) -> p c t", c=4)
                ts(edge[:, 0:4], bx[:, :, P - 1], k16, None, MUL, s="edge")
                ts(edge[:, 4:5], bF[:, N - 1:N], k16, None, MUL, s="edge")
                ts(edge[:, 5:9], nx[:, :, 0], -k16, None, MUL, s="edge")
                ts(edge[:, 9:10], nB[:, T:T + 1], -k16, None, MUL, s="edge")

                def exponents(l):
                    b = LEVELS[l - 1]
                    f, n_ = (x[:, 0:T].rearrange("p (n s b) -> p n s b", s=2, b=b) for x in (bF, nB))
                    eq, ek = (level_ex[l % 3][:, i, :].rearrange("p (n s b) -> p n s b", s=2, b=b) for i in range(2))
                    shape = [P, T // (2 * b), b]
                    fm = f[:, :, 0, b - 1:b].to_broadcast(shape)
                    nm = n_[:, :, 1, 0:1].to_broadcast(shape)
                    tt(eq[:, :, 1, :], f[:, :, 1, :], fm, SUB, "le")
                    tt(ek[:, :, 0, :], fm, f[:, :, 0, :], SUB, "le")
                    tt(eq[:, :, 0, :], nm, n_[:, :, 0, :], SUB, "le")
                    tt(ek[:, :, 1, :], n_[:, :, 1, :], nm, SUB, "le")

                def masked(l):
                    ps = psum(("lev", h, l))
                    m = masks[:, l:l + 1, :].to_broadcast([P, 4, P])
                    src = ps[:, 0:T].rearrange("p (c t) -> p c t", c=4)
                    dst = (Am if l else At)[:, :].rearrange("p (c t) -> p c t", c=4)
                    if l and h + l > 1:
                        ve.wait_ge(sem("ladd"), 7 * h + l - 1)
                    tt(dst, src, m, MUL, "lev")

                ve.wait_ge(sem("glc"), 32)
                exponents(1)
                masked(0)
                ve.wait_ge(sem("gk"), h + 1)
                for l in range(1, 8):
                    if l < 7:
                        if l > 2:
                            psum(("lev", h, l - 2))
                        exponents(l + 1)
                    ve.wait_ge(sem("lx"), 7 * h + l)
                    for i, x in enumerate([gq[:, :], gk[:, 0:T]]):
                        tt(level_ex[l % 3][:, i, :], level_ex[l % 3][:, i, :], x, MUL, "lq")
                    if l >= 2:
                        masked(l - 1)
                masked(7)
                for d in range(2):
                    ve.wait_ge(sem("kx"), 11 * h + 6 + 5 * d)
                    e = ex[:, d, :, :].rearrange("p a t -> p (a t)")
                    tt(e[:, 0:N], e[:, 0:N], gk[:, :], MUL, "kd")
                for j in range(2):
                    ve.wait_ge(sem("qx"), 2 * h + j + 1)
                    tt(ex[:, 0, j, :], ex[:, 0, j, :], gq[:, :], MUL, "qd")
                for i in range(2):
                    if i == 0:
                        ps = psum(("st", h, 0))
                        do(nc.vector.tensor_copy(S[:, 0, 0, :], ps[:, 0:GV]), "st")
                        for c in range(3):
                            stt(S[:, 0, c + 1, :], S[:, 0, c, :], edge[:, 10 + c:11 + c], ps[:, (c + 1) * GV:(c + 2) * GV],
                                MUL, ADD, "st")
                    else:
                        ps = psum(("st", h, 1))
                        do(nc.vector.tensor_copy(S[:, 1, 3, :], ps[:, 0:GV]), "st")
                        for n, c in enumerate([3, 2, 1]):
                            stt(S[:, 1, c - 1, :], S[:, 1, c, :], edge[:, 15 + c:16 + c], ps[:, (n + 1) * GV:(n + 2) * GV],
                                MUL, ADD, "st")
                sums(f"o{h}")
                if h + 1 < GH:
                    decay(h + 1, 0)
                ve.wait_ge(sem("gs"), h + 1)
                apply(f"o{h}", lambda k: ex[:, 1, k, :], lambda k: v_("o_g", k), lambda k: ghi[:, 2 * h + k, :],
                      lambda k: glo[:, 2 * h + k, :], T, lambda k: gG[:, k, :])
                if h + 1 < GH:
                    decay(h + 1, 1)
            def col(i):
                return sp[:, i, :]

            ve.wait_ge(sem("s5c"), 16 * 3)
            lr, li = col(0), v_("lam_im", 0, 8)
            ts(lr, v_("lam_re", 0, 8), -1e-4, None, MIN, s="sp_a")
            ve.wait_ge(sem("sp_b"), 1)
            tt(col(4), li, col(1), MUL)
            tt(col(2), lr, col(1), MUL, "sp_a")
            big = 1.5 * 2.0 ** 23
            ts(col(5), col(4), float(1.0 / (2.0 * np.pi)), big, MUL, ADD)
            ts(col(5), col(5), big, None, SUB)
            c1, c2 = 6.28125, float(np.float32(2.0 * np.pi - 6.28125))
            c3 = float(2.0 * np.pi - 6.28125 - c2)
            stt(col(6), col(5), -c1, col(4), MUL, ADD)
            stt(col(6), col(5), -c2, col(6), MUL, ADD)
            stt(col(6), col(5), -c3, col(6), MUL, ADD)
            pi = 3.1415925
            ts(col(6), col(6), pi, -pi, MIN, MAX)
            ts(col(9), col(6), 0.5, None, MUL, s="sp_a")
            for m in range(2):
                resid(("l1", m), m, mod[:, 1, 32 + 2 * m:33 + 2 * m])
            ve.wait_ge(sem("sp_b"), 4)
            tt(col(10), col(8), col(8), MUL)
            ts(col(10), col(10), -2.0, 1.0, MUL, ADD)
            tt(col(11), col(3), col(10), MUL)
            ts(col(11), col(11), -1.0, None, ADD)
            tt(col(12), col(3), col(7), MUL)
            tt(col(13), lr, lr, MUL)
            tt(col(14), li, li, MUL)
            tt(col(13), col(13), col(14), ADD)
            do(nc.vector.reciprocal(col(13), col(13)))
            tt(col(15), col(11), lr, MUL)
            tt(col(16), col(12), li, MUL)
            tt(col(15), col(15), col(16), ADD)
            tt(col(15), col(15), col(13), MUL)
            tt(col(16), col(12), lr, MUL)
            tt(col(17), col(11), li, MUL)
            tt(col(16), col(16), col(17), SUB)
            tt(col(16), col(16), col(13), MUL)
            for m in range(2, 4):
                resid(("l1", m), m, mod[:, 1, 32 + 2 * m:33 + 2 * m])
            zr, zi = (sp[:, i, :].rearrange("p (g o) -> p g o", o=1).to_broadcast([P, SG, 32]) for i in (15, 16))
            t0, t1, t2 = (tmp[:, 0, i * 256:(i + 1) * 256].rearrange("p (g o) -> p g o", o=32) for i in range(3))
            tt(t0, lC[:, 0, :, :], zr, MUL)
            tt(t1, lC[:, 1, :, :], zi, MUL)
            tt(t0, t0, t1, SUB)
            tt(t1, lC[:, 0, :, :], zi, MUL)
            tt(t2, lC[:, 1, :, :], zr, MUL)
            do(nc.vector.tensor_copy(lC[:, 0, :, :], t0), "lZ")
            stt(lC[:, 1, :, :], t1, -1.0, t2, MUL, SUB, "lZ")
            for m in range(4, 6):
                resid(("l1", m), m, mod[:, 1, 32 + 2 * m:33 + 2 * m])
            do(nc.vector.tensor_copy(tab[:, 0, :, 0], col(10)))
            do(nc.vector.tensor_copy(tab[:, 1, :, 0], col(7)))
            for b in LEVELS:
                shape = [P, SG, b]
                cm, sm = (tab[:, i, :, b - 1:b].to_broadcast(shape) for i in range(2))
                cs, sn = (tab[:, i, :, 0:b] for i in range(2))
                t0, t1 = (tmp[:, 0, i * 512:i * 512 + SG * b].rearrange("p (g o) -> p g o", g=SG) for i in range(2))
                tt(t0, cs, cm, MUL)
                tt(t1, sn, sm, MUL)
                tt(tab[:, 0, :, b:2 * b], t0, t1, SUB)
                tt(t0, cs, sm, MUL)
                tt(t1, sn, cm, MUL)
                tt(tab[:, 1, :, b:2 * b], t0, t1, ADD, "tab")
            for m in range(6, 8):
                resid(("l1", m), m, mod[:, 1, 32 + 2 * m:33 + 2 * m])
            do(nc.vector.tensor_copy(step.rearrange("p (g t) -> p g t", g=SG), sp[:, 3, :].rearrange("p (g o) -> p g o", o=1).to_broadcast([P, SG, P])))
            do(nc.vector.memset(step.rearrange("p (g t) -> p g t", g=SG)[:, :, 0], 0.0))
            sums("f1")
            ve.wait_ge(sem("n_rs"), 2 * NI["f1"] + 2)
            for k in range(KD):
                stt(X[:, k, :], X[:, k, :], v_("final_g", k), rstd[:, 0:T], MUL, MUL, "resid")
            ts(small2[:, 0:1], eps1[:, 0:1], 1.0, None, MUL, s="n_use")
            sums("mix0")
            apply("mix0", lambda k: X[:, k, :], lambda k: v_("mix_g0", k), lambda k: Ahi[:, k, 0:T],
                  lambda k: Alo[:, k, 0:T], T)

            def rotate(x, j, back):
                a_, b_ = (y.rearrange("p (i c t) -> p i c t", i=2, t=P) for y in (tmp[:, 1, :], wtmp))
                cs, sn = (tab[:, i, j:j + 1, :].to_broadcast([P, TX, P]) for i in range(2))
                re, im = wS[:, :, 0, j, :], wS[:, :, 1, j, :]
                if back:
                    for i, y in enumerate((re, im)):
                        tt(a_[:, i], y, cs, MUL)
                        tt(b_[:, i], y, sn, MUL)
                else:
                    cs, sn = (tab[:, i, j:j + 1, :].to_broadcast([P, 2 * TX, P]) for i in range(2))
                    flat = lambda y: y.rearrange("p i c t -> p (i c) t")
                    tt(flat(a_), x.rearrange("p (c t) -> p c t", t=P), cs, MUL)
                    tt(flat(b_), x.rearrange("p (c t) -> p c t", t=P), sn, MUL, "sx")
                tt(re, a_[:, 0], b_[:, 1], SUB if back else ADD)
                tt(im, a_[:, 1], b_[:, 0], ADD if back else SUB, "sh" if back else None)

            for j in range(SG):
                rotate(psum(("sx", j))[:, :], j, False)
            for c in range(TX):
                for i in range(2):
                    x = wS[:, c, i, :, :].rearrange("p g t -> p (g t)")
                    do(nc.vector.tensor_tensor_scan(x, step, x, 0.0, MUL, ADD), "scan" if c == TX - 1 and i else None)
                if c == 1:
                    ve.wait_ge(sem("mv_rs"), 1)
                    for t in range(TX):
                        ts(mV[:, t, :], mV[:, t, :], mst[:, t:t + 1], None, MUL, s="mvn")
                if c < TX - 1:
                    gr, gi = (wS[:, c, i, :, P - 1] for i in range(2))
                    ct, st_ = (tab[:, i, :, P - 1] for i in range(2))
                    tt(col(26), gr, ct, MUL)
                    tt(col(27), gi, st_, MUL)
                    tt(col(24), col(26), col(27), SUB)
                    tt(col(26), gi, ct, MUL)
                    tt(col(27), gr, st_, MUL)
                    tt(col(25), col(26), col(27), ADD)
                    for i in range(2):
                        first = wS[:, c + 1, i, :, 0]
                        tt(col(26), col(24 + i), col(3), MUL)
                        tt(first, first, col(26), ADD)
            for j in range(BACK):
                rotate(None, j, True)
            for m in range(GM):
                ps = psum(("mg", m))
                v4 = lambda y: y.rearrange("p (c t) -> p c t", c=4)
                stt(v4(tmp[:, 1, 0:T]), v4(ps[:, 0:T]), v_("v_g", m), bs[:, m:m + 1, :].to_broadcast([P, 4, P]), MUL, ADD, "mg")
                ve.wait_ge(sem("mu"), m + 1)
                b = to_split(T)
                tt(b, tmp[:, 1, 0:T], mU[:, m, :], MUL, "hf")
                queued(Ahi[:, 2 + m, 0:T], Alo[:, 2 + m, 0:T])
            flush()
            for c in range(2):
                ps = psum(("sy", c))
                stt(U[:, c, :], U[:, c, :], v_("s5_d", c), ps[:, 0:T], MUL, ADD, "sy")
            for c in range(2):
                ve.wait_ge(sem("glu"), c + 1)
                e = tmp[:, 1, c * T:(c + 1) * T]
                b = to_split(T)
                tt(b, e, U[:, c, :], MUL, "hf")
                queued(Ahi[:, c, 0:T], Alo[:, c, 0:T])
            flush()
            for m in range(8):
                resid(("ev", m), m)

            def ffn(l):
                sums(f"ffn{l}")
                apply(f"ffn{l}", lambda k: X[:, k, :], lambda k: v_(f"ffn_g{l}", k), lambda k: Ahi[:, k, 0:T],
                      lambda k: Alo[:, k, 0:T], T)
                for f in range(2):
                    for r_ in range(FH + 1):
                        if r_ < FH:
                            ps = psum(("up", l, f, r_))
                            j = (2 * l + f) * FH + r_
                            for part in range(2):
                                ve.wait_ge(sem("ca"), 2 * j + part + 1)
                                c = (part * 2 + f) * FH + r_
                                for back in (1, 2):
                                    y = cv[:, j % 3, part, back:T]
                                    stt(y, ps[:, part * T:part * T + T - back], v_(f"ffn_w{l}", 44 * (2 - back) + c), y,
                                        MUL, ADD, "conv")
                        if r_:
                            j = (2 * l + f) * FH + r_ - 1
                            ve.wait_ge(sem("se"), j + 1)
                            e = tmp[:, j % 2, 0:T]
                            b = to_split(T)
                            tt(b, e, cv[:, j % 3, 1, :], MUL, "hf")
                            queued(Fhi[:, r_ - 1, :], Flo[:, r_ - 1, :])
                    flush()
                    for m in range(8):
                        resid(("dn", l, f, m), m)

            ffn(0)
            sums("mix1")
            apply("mix1", lambda k: X[:, k, :], lambda k: v_("mix_g1", k), lambda k: Ahi[:, k, 0:T],
                  lambda k: Alo[:, k, 0:T], T)
            for r_ in range(9):
                if r_ < 8:
                    ps = psum(("ch", r_))
                    ve.wait_ge(sem("oc"), r_ + 1)
                    tt(cv[:, r_ % 3, 1, :], cv[:, r_ % 3, 0, :], ps[:, T:2 * T], MUL, "ch")
                if r_:
                    m = r_ - 1
                    ve.wait_ge(sem("oa"), m + 1)
                    ps = psum(("bg", m))
                    for back in (1, 2):
                        y = tmp[:, m % 2, back:T]
                        stt(y, cv[:, m % 3, 1, 0:T - back], v_("od_w", 8 * (2 - back) + m), y, MUL, ADD)
                    b = to_split(T)
                    tt(b, tmp[:, m % 2, 0:T], ps[:, 0:T], MUL, "hf")
                    queued(Fhi[:, m, :], Flo[:, m, :])
            flush()
            for m in range(8):
                resid(("od", m), m)
            ffn(1)
            sums("f2")
            ve.wait_ge(sem("n_rs"), 2 * NI["f2"] + 2)
            for k in range(KD):
                stt(X[:, k, :], X[:, k, :], v_("final_g2", k), rstd[:, 0:T], MUL, MUL, "out")


def _swap(w):
    return np.concatenate([w[..., 8:16], w[..., 0:8], w[..., 24:32], w[..., 16:24]], -1)


def _matrices(w):
    z = lambda *s: np.zeros(s, np.float32)
    m = {}
    wi = w["mla_w_in"][0]
    kr = wi[:, QR + KVR:QR + KVR + ROPE]
    m["win0"] = np.concatenate([wi[:, :QR + KVR], z(D, 64), kr, _swap(kr), wi[:, QR + KVR + ROPE:]], 1)
    uq = w["mla_w_uq"][0].reshape(QR, H, NOPE + ROPE)
    m["uq"] = np.concatenate([uq, _swap(uq[..., NOPE:])], -1).reshape(QR, H * P)
    ukv = w["mla_w_ukv"][0].reshape(KVR, H, NOPE + HV)
    m["uk"] = np.concatenate([ukv[..., :NOPE], z(KVR, H, P - NOPE)], -1).reshape(KVR, H * P)
    m["uv"] = ukv[..., NOPE:].reshape(KVR, H * HV)
    m["wout0"], m["wout1"] = w["mla_w_out"][0], w["gla_w_out"][0]
    gi = w["gla_w_in"][0]
    m["gin"] = gi[:, :3 * D]
    m["gr"] = np.concatenate([gi[:, 3 * D:], z(D, P - 32)], 1)
    m["ein"], m["eout"] = w["ev_w_in_2"][0], w["ev_w_out_2"][0]
    m["oin"], m["oout"] = w["od_w_in_2"][0], w["od_w_out_2"][0]
    for l in range(2):
        m[f"up{l}"], m[f"dn{l}"] = w["ffn_w_up_2"][l], w["ffn_w_down_2"][l]
    return m


def _columns(v):
    return np.asarray(v).reshape(-1, P).T


def _arrays(w):
    w = {k: np.asarray(v) for k, v in w.items()}
    mats = _matrices(w)
    units = np.zeros((len(PLAN.units), P, UT, P), np.float32)
    for c, (kind, i) in enumerate(PLAN.units):
        for j in range(UT):
            if kind == "raw":
                units[c, :, j, :] = w["ada_w"][i // 24][j * P:(j + 1) * P, i % 24 * P:(i % 24 + 1) * P]
            elif i * UT + j < len(PLAN.split):
                name, k, m = PLAN.split[i * UT + j]
                units[c, :, j, :] = mats[name][k * P:(k + 1) * P, m * P:(m + 1) * P]
    twice = lambda v: np.repeat(_columns(v), 2, 1)
    parts = {
        "cond": np.stack([_columns(w["c"][0]), _columns(w["c_ctx"])], 2).reshape(P, 16),
        "ada_b0": twice(w["ada_b"][0]), "ada_b1": twice(w["ada_b"][1]),
        "norm_g0": twice(w["norm_g"][0]), "norm_g1": twice(w["norm_g"][1]),
        "final_g": _columns(w["final_g"]), "q_g": _columns(w["mla_q_norm"][0]),
        "kv_g": _columns(w["mla_kv_norm"][0]), "b_gf": _columns(w["gla_b_gf"][0]),
        "b_gb": _columns(w["gla_b_gb"][0]), "o_g": _columns(w["gla_o_norm"][0]),
        "mix_g0": _columns(w["mix_norm_g_2"][0]), "mix_g1": _columns(w["mix_norm_g_2"][1]),
        "ffn_g0": _columns(w["ffn_norm_g_2"][0]), "ffn_g1": _columns(w["ffn_norm_g_2"][1]),
        "final_g2": _columns(w["final_norm_g_2"]),
        "lam_re": _columns(w["s5_lam_re_2"][0]), "lam_im": _columns(w["s5_lam_im_2"][0]),
        "log_dt": _columns(np.repeat(w["s5_log_dt_2"][0], 64)),
        "s5_d": _columns(w["s5_d_2"][0]), "b_glu": _columns(w["s5_b_glu_2"][0]),
        "v_g": _columns(w["gm_v_g_2"][0]), "od_w": _columns(w["od_conv_w_2"][0]),
        "od_b": _columns(w["od_conv_b_2"][0]),
        "ffn_w0": _columns(w["ffn_conv_w_2"][0]), "ffn_w1": _columns(w["ffn_conv_w_2"][1]),
        "ffn_b0": _columns(w["ffn_conv_b_2"][0]), "ffn_b1": _columns(w["ffn_conv_b_2"][1]),
    }
    vec = np.concatenate([parts[n] for n, _ in VECS], 1)
    assert vec.shape == (P, NV)
    t = np.arange(T)
    inv = np.float32(10000.0) ** (-np.arange(8, dtype=np.float32) / np.float32(8))
    ang = [(pos.astype(np.float32)[None, :] * inv[:, None]).astype(np.float32) for pos in (t // 64, t % 64)]
    cos, sin = [np.cos(x) for x in ang], [np.sin(x) for x in ang]
    rope = np.zeros((P, T), np.float32)
    rope[64:96] = np.concatenate([cos[0], cos[0], cos[1], cos[1]])
    rope[96:128] = np.concatenate([-sin[0], sin[0], -sin[1], sin[1]])
    wg = np.zeros((32, 2, 512), np.float32)
    wg[0:16, 0], wg[16:32, 1] = w["gla_w_gf"][0], w["gla_w_gb"][0]
    i = np.arange(P)
    masks = np.zeros((P, 8, P), np.float32)
    masks[:, 0] = 2.0 * (i[:, None] == i[None, :])
    for l, b in enumerate(LEVELS):
        masks[:, l + 1] = (i[:, None] // (2 * b) == i[None, :] // (2 * b)) & (i[:, None] // b != i[None, :] // b)
    lB, lC = np.zeros((P, 2, 2, P), np.float32), np.zeros((P, 2, SG, 32), np.float32)
    for j in range(SG):
        for g in range(2):
            for r, (b, c) in enumerate([("s5_b_re_2", "s5_c_re_2"), ("s5_b_im_2", "s5_c_im_2")]):
                at = 32 * (j % 4) + 16 * g
                lB[at:at + 16, j // 4, r, 64 * g:64 * g + 64] = w[b][0, 2 * j + g].T
                lC[64 * g:64 * g + 64, r, j, 16 * g:16 * g + 16] = w[c][0, 2 * j + g].T
    eps1 = np.zeros((P, 2), np.float32)
    eps1[:, 0], eps1[:, 1] = EPS, 1.0
    return {
        "units": units.reshape(len(PLAN.units), P, UT * P), "vec": vec, "rope": rope, "eps1": eps1,
        "ident": np.eye(P, dtype=np.float32), "wg": wg, "masks": masks, "lB": lB, "lC": lC,
        "xT": w["x"][0].T.reshape(KD, P, T).transpose(1, 0, 2),
        "ctxT": w["ctx"][0].T.reshape(KD, P, TC).transpose(1, 0, 2),
        "glw": w["s5_w_glu_2"][0].reshape(2, P, SW).transpose(1, 0, 2),
        "gmw": w["gm_w_s_2"][0].transpose(2, 0, 1),
        "bs": np.broadcast_to(w["gm_b_s_2"][0][None], (P, GM, P)),
    }


def kernel(**inputs):
    import concourse.bacc as bacc
    from concourse.bass_utils import run_bass_kernel_spmd

    nc = bacc.Bacc("TRN2", target_bir_lowering=False, num_devices=1, dynamic_dma_scratch_size=64)
    arrays = {f"in_{k}": np.ascontiguousarray(v) for k, v in _arrays(inputs).items()}
    a = {k[3:]: nc.dram_tensor(k, v.shape, mybir.dt.float32, kind="ExternalInput").ap() for k, v in arrays.items()}
    a["out"] = nc.dram_tensor("out_xT", (P, KD, T), mybir.dt.float32, kind="ExternalOutput").ap()
    build(nc, a)
    r = run_bass_kernel_spmd(nc, [arrays], core_ids=[0])
    got = r.results[0]["out_xT"]
    return got.transpose(1, 0, 2).reshape(D, T).T[None]
```
